# Optimizing a Trainium2 kernel written in Bass

```python
import jax, jax.numpy as jnp
from jax import lax
import numpy as np

D_MODEL = 1024
BATCH = 1
SEQ = 512
DEPTH = 2
DEC_BATCH = 8
DEC_SEQ = 8
PAST_LEN = 4096
PAGE_SIZE = 128

N_MIXERS = 2
N_A_LAYERS = (DEPTH + 1) // 2
N_B_LAYERS = DEPTH // 2
CHUNK = 128
A_HEADS = 4
A_WIDTH = 3 * D_MODEL
A_HEAD_DIM = A_WIDTH // A_HEADS
CONV_WIDTH = 3
B_WIDTH = D_MODEL
N_GROUPS = 4
EXPERTS_PER_GROUP = 4
N_EXPERTS = N_GROUPS * EXPERTS_PER_GROUP
TOP_K_INNER = 2
D_EXPERT = D_MODEL // 4
PLE_DIM = 256
LN_EPS = 1e-5
DEEPNORM_ALPHA = (2 * DEPTH) ** 0.25
DEEPNORM_BETA = (8 * DEPTH) ** -0.25

kernel_name = "hybrid_chunkgmlp_shortconv_hmoe_step"

def layer_norm(x, g, b):
    xf = x.astype(jnp.float32)
    mu = jnp.mean(xf, axis=-1, keepdims=True)
    var = jnp.mean(jnp.square(xf - mu), axis=-1, keepdims=True)
    y = (xf - mu) * lax.rsqrt(var + LN_EPS)
    return (y * g.astype(jnp.float32) + b.astype(jnp.float32)).astype(x.dtype)

def chunk_spatial_gate(v, w_s, b_s):
    bsz, s, _ = v.shape
    n_chunks = -(-s // CHUNK)
    pad = n_chunks * CHUNK - s
    vp = jnp.pad(v, ((0, 0), (0, pad), (0, 0))).reshape(bsz, n_chunks, CHUNK, A_HEADS, A_HEAD_DIM)
    causal = jnp.tril(jnp.ones((CHUNK, CHUNK), dtype=bool))
    w_masked = jnp.where(causal[None], w_s, jnp.zeros((), w_s.dtype))
    out = jnp.einsum("hts,bcshd->bcthd", w_masked, vp) + jnp.transpose(b_s)[:, :, None]
    return out.reshape(bsz, n_chunks * CHUNK, A_WIDTH)[:, :s]

def chunk_gmlp_mixer(x, w_in, b_in, ln_g, ln_b, w_s, b_s, w_out):
    z = jax.nn.gelu(jnp.einsum("bsd,de->bse", x, w_in) + b_in, approximate=False)
    u, v = jnp.split(z, 2, axis=-1)
    v = layer_norm(v, ln_g, ln_b)
    sg = chunk_spatial_gate(v, w_s, b_s)
    y = jnp.einsum("bse,ed->bsd", u * sg, w_out)
    return y, v

def short_conv_mixer(x, past, w_in, conv_w, w_out):
    s = x.shape[1]
    h = jnp.einsum("bsd,de->bse", x, w_in)
    gate_b, gate_c, hx = jnp.split(h, 3, axis=-1)
    hp = jnp.concatenate([past, gate_c * hx], axis=1)
    conv = conv_w[0] * hp[:, 0:s]
    for k in range(1, CONV_WIDTH):
        conv = conv + conv_w[k] * hp[:, k:k + s]
    y = jnp.einsum("bse,ed->bsd", gate_b * conv, w_out)
    return y, hp[:, s:]

def hier_moe(x, w_group, b_group, w_expert, b_expert, w_gate_up, w_down):
    bsz, s, d = x.shape
    xt = x.reshape(-1, d)
    g_logits = (xt @ w_group + b_group).astype(jnp.float32)
    g_probs = jax.nn.softmax(g_logits, axis=-1)
    g_idx = jnp.argmax(g_logits, axis=-1)
    g_w = jnp.take_along_axis(g_probs, g_idx[:, None], axis=-1)[:, 0]
    e_logits = (xt @ w_expert + b_expert).astype(jnp.float32).reshape(-1, N_GROUPS, EXPERTS_PER_GROUP)
    e_in_group = jnp.take_along_axis(e_logits, g_idx[:, None, None], axis=1)[:, 0]
    top_vals, top_idx = lax.top_k(e_in_group, TOP_K_INNER)
    top_w = jax.nn.softmax(top_vals, axis=-1) * g_w[:, None]
    expert_id = g_idx[:, None] * EXPERTS_PER_GROUP + top_idx
    combine = jnp.sum(jax.nn.one_hot(expert_id, N_EXPERTS, dtype=jnp.float32) * top_w[..., None], axis=1)
    hgu = jnp.einsum("td,edf->tef", xt, w_gate_up)
    gate, up = jnp.split(hgu, 2, axis=-1)
    a = jax.nn.silu(gate) * up * combine.astype(x.dtype)[:, :, None]
    y = jnp.einsum("tef,efd->td", a, w_down)
    return y.reshape(bsz, s, d)

def run_trunk(x, p, conv_past, a_w_in, a_b_in, a_ln_g, a_ln_b, a_w_s, a_b_s, a_w_out,
              b_w_in, b_conv_w, b_w_out, ln1_g, ln1_b, ln2_g, ln2_b,
              moe_w_group, moe_b_group, moe_w_expert, moe_b_expert, moe_w_gate_up, moe_w_down,
              ple_w_gate, ple_b_gate, ple_w_proj):
    v_states = []
    conv_states = []
    s = x.shape[1]
    open_start = ((s - 1) // CHUNK) * CHUNK
    for i in range(DEPTH):
        j = i // N_MIXERS
        if i % N_MIXERS == 0:
            mix, v = chunk_gmlp_mixer(x, a_w_in[j], a_b_in[j], a_ln_g[j], a_ln_b[j], a_w_s[j], a_b_s[j], a_w_out[j])
            v_states.append(v[:, open_start:])
        else:
            mix, buf = short_conv_mixer(x, conv_past[j], b_w_in[j], b_conv_w[j], b_w_out[j])
            conv_states.append(buf)
        x = layer_norm(DEEPNORM_ALPHA * x + mix, ln1_g[i], ln1_b[i])
        moe = hier_moe(x, moe_w_group[i], moe_b_group[i], moe_w_expert[i], moe_b_expert[i],
                       moe_w_gate_up[i], moe_w_down[i])
        x = layer_norm(DEEPNORM_ALPHA * x + moe, ln2_g[i], ln2_b[i])
        gate = jax.nn.sigmoid(jnp.einsum("bsd,de->bse", x, ple_w_gate[i]) + ple_b_gate[i])
        x = x + gate * jnp.einsum("bsp,pd->bsd", p[i], ple_w_proj[i])
    return x, jnp.stack(v_states), jnp.stack(conv_states)

def setup_inputs(seed: int = 0) -> dict:
    key = jax.random.key(seed)
    ks = jax.random.split(key, 32)
    f32 = jnp.float32

    def nrm(k, shape, scale):
        return jax.random.normal(k, shape, f32) * scale

    return {
        "x_prompt": nrm(ks[0], (BATCH, SEQ, D_MODEL), 1.0),
        "x_sample": nrm(ks[1], (DEC_BATCH, DEC_SEQ, D_MODEL), 1.0),
        "state_conv": nrm(ks[2], (N_B_LAYERS, DEC_BATCH, CONV_WIDTH - 1, B_WIDTH), 1.0),
        "p_prompt": nrm(ks[3], (DEPTH, BATCH, SEQ, PLE_DIM), 1.0),
        "p_sample": nrm(ks[4], (DEPTH, DEC_BATCH, DEC_SEQ, PLE_DIM), 1.0),
        "a_w_in": nrm(ks[5], (N_A_LAYERS, D_MODEL, 2 * A_WIDTH), D_MODEL ** -0.5),
        "a_b_in": nrm(ks[6], (N_A_LAYERS, 2 * A_WIDTH), 0.02),
        "a_ln_g": 1.0 + nrm(ks[7], (N_A_LAYERS, A_WIDTH), 0.05),
        "a_ln_b": nrm(ks[8], (N_A_LAYERS, A_WIDTH), 0.02),
        "a_w_s": nrm(ks[9], (N_A_LAYERS, A_HEADS, CHUNK, CHUNK), 0.5 * CHUNK ** -0.5),
        "a_b_s": 1.0 + nrm(ks[10], (N_A_LAYERS, A_HEADS, CHUNK), 0.1),
        "a_w_out": nrm(ks[11], (N_A_LAYERS, A_WIDTH, D_MODEL), DEEPNORM_BETA * A_WIDTH ** -0.5),
        "b_w_in": nrm(ks[12], (N_B_LAYERS, D_MODEL, 3 * B_WIDTH), D_MODEL ** -0.5),
        "b_conv_w": nrm(ks[13], (N_B_LAYERS, CONV_WIDTH, B_WIDTH), CONV_WIDTH ** -0.5),
        "b_w_out": nrm(ks[14], (N_B_LAYERS, B_WIDTH, D_MODEL), DEEPNORM_BETA * B_WIDTH ** -0.5),
        "ln1_g": 1.0 + nrm(ks[15], (DEPTH, D_MODEL), 0.05),
        "ln1_b": nrm(ks[16], (DEPTH, D_MODEL), 0.02),
        "ln2_g": 1.0 + nrm(ks[17], (DEPTH, D_MODEL), 0.05),
        "ln2_b": nrm(ks[18], (DEPTH, D_MODEL), 0.02),
        "moe_w_group": nrm(ks[19], (DEPTH, D_MODEL, N_GROUPS), D_MODEL ** -0.5),
        "moe_b_group": nrm(ks[20], (DEPTH, N_GROUPS), 0.01),
        "moe_w_expert": nrm(ks[21], (DEPTH, D_MODEL, N_EXPERTS), D_MODEL ** -0.5),
        "moe_b_expert": nrm(ks[22], (DEPTH, N_EXPERTS), 0.01),
        "moe_w_gate_up": nrm(ks[23], (DEPTH, N_EXPERTS, D_MODEL, 2 * D_EXPERT), D_MODEL ** -0.5),
        "moe_w_down": nrm(ks[24], (DEPTH, N_EXPERTS, D_EXPERT, D_MODEL), DEEPNORM_BETA * D_EXPERT ** -0.5),
        "ple_w_gate": nrm(ks[25], (DEPTH, D_MODEL, D_MODEL), D_MODEL ** -0.5),
        "ple_b_gate": nrm(ks[26], (DEPTH, D_MODEL), 0.02),
        "ple_w_proj": nrm(ks[27], (DEPTH, PLE_DIM, D_MODEL), DEEPNORM_BETA * PLE_DIM ** -0.5),
    }

def reference(x_prompt, x_sample, state_conv, p_prompt, p_sample,
              a_w_in, a_b_in, a_ln_g, a_ln_b, a_w_s, a_b_s, a_w_out,
              b_w_in, b_conv_w, b_w_out, ln1_g, ln1_b, ln2_g, ln2_b,
              moe_w_group, moe_b_group, moe_w_expert, moe_b_expert, moe_w_gate_up, moe_w_down,
              ple_w_gate, ple_b_gate, ple_w_proj):
    conv_zero = jnp.zeros((N_B_LAYERS, x_prompt.shape[0], CONV_WIDTH - 1, B_WIDTH), x_prompt.dtype)
    y_prompt, state_chunk_v_prompt, state_conv_prompt = run_trunk(
        x_prompt, p_prompt, conv_zero, a_w_in, a_b_in, a_ln_g, a_ln_b, a_w_s, a_b_s, a_w_out,
        b_w_in, b_conv_w, b_w_out, ln1_g, ln1_b, ln2_g, ln2_b,
        moe_w_group, moe_b_group, moe_w_expert, moe_b_expert, moe_w_gate_up, moe_w_down,
        ple_w_gate, ple_b_gate, ple_w_proj)
    y_sample, state_chunk_v_sample, state_conv_sample = run_trunk(
        x_sample, p_sample, state_conv, a_w_in, a_b_in, a_ln_g, a_ln_b, a_w_s, a_b_s, a_w_out,
        b_w_in, b_conv_w, b_w_out, ln1_g, ln1_b, ln2_g, ln2_b,
        moe_w_group, moe_b_group, moe_w_expert, moe_b_expert, moe_w_gate_up, moe_w_down,
        ple_w_gate, ple_b_gate, ple_w_proj)
    return (y_prompt, y_sample, state_chunk_v_prompt, state_chunk_v_sample, state_conv_prompt, state_conv_sample)


_drawn_inputs = setup_inputs


def setup_inputs(seed=0):
    import zlib

    import numpy as np

    out = dict(_drawn_inputs(seed))
    spreads = {}
    factors = {'a_ln_b': 2.884, 'moe_b_group': 24.546, 'moe_b_expert': 20.254, 'ple_b_gate': 8.0}
    for name, (base, spread) in spreads.items():
        noise = np.random.default_rng([zlib.crc32(name.encode()), seed]).standard_normal(out[name].shape)
        drawn = base * np.exp(spread * noise) if base else spread * noise
        out[name] = __import__('jax').numpy.asarray(drawn.astype(out[name].dtype))
    for name, factor in factors.items():
        out[name] = (out[name] * factor).astype(out[name].dtype)
    return out
```

```python
import concourse.bass as bass
from concourse import mybir
from contextlib import ExitStack

P = 128
D = 1024
KT = D // P
TP, TS = 512, 64
T = TP + TS
NT = 5
HALF = T // 2
AW = 3072
NH = 4
NE = 16
F = 256
PLE = 256
RB, SB = 8, 8
DEPTH = 2
EPS = 1e-5
ALPHA = float((2 * DEPTH) ** 0.25)
UNIT = 2048
CAP = 128
OVF = 8
SLOT_TILES = NE + OVF
ROUND = 4
AR = AW // P // ROUND
BR = KT // ROUND
VU = AW // 256
U_V = 0
U_A = U_V + VU
U_P = [U_A + 4 * AR, 0]
U_E = [U_P[0] + 4, 0]
EU = 3 * NE
U_G = [U_E[0] + EU, 0]
U_CH = U_G[0] + 4
U_B = U_CH + 8
U_P[1] = U_B + 4 * BR
U_E[1] = U_P[1] + 4
U_G[1] = U_E[1] + EU
U_END = U_G[1] + 4
M_A = 0
M_P = [12 * AR, 0]
M_G = [M_P[0] + 8, 0]
M_CH = M_G[0] + 8
M_B = M_CH + 16
M_P[1] = M_B + 12 * BR
M_G[1] = M_P[1] + 8
AHEAD = 3


class Chain:

    def __init__(self, eng, sem):
        self.eng, self.sem, self.base, self.k, self.it, self.per = eng, sem, 0, 0, 0, 0

    def enter(self, it, per):
        self.base, self.it, self.per, self.k = self.base + self.k, it, per, 0

    def leave(self, n):
        assert self.k == self.per, (self.k, self.per)
        self.base, self.k, self.it, self.per = self.base + self.per * n, 0, 0, 0

    def link(self, ins):
        self.k += 1
        ins.then_inc(self.sem, 1)
        self.eng.wait_ge(self.sem, self.base + self.k + (self.it * self.per if self.per else 0))


def trunk(nc, x_in, outs):
    f32, f32r, i32, u32 = mybir.dt.float32, mybir.dt.float32r, mybir.dt.int32, mybir.dt.uint32
    ACT, ALU, AX = mybir.ActivationFunctionType, mybir.AluOpType, mybir.AxisListType
    ds = bass.ds

    x_prompt = x_in["x_prompt"][0].rearrange("(i p) d -> p i d", p=P)
    x_sample = x_in["x_sample"].rearrange("b s d -> (b s) d")
    w_in = x_in["a_w_in"][0]
    w_out = x_in["a_w_out"][0]
    bw_in = x_in["b_w_in"][0]
    bw_out = x_in["b_w_out"][0]
    v_dram = nc.dram_tensor("v_scratch", (NT, P, AW), f32).ap()
    x_dram = [nc.dram_tensor(f"x_scratch{l}", (T, D), f32).ap() for l in range(DEPTH)]
    y_dram = [nc.dram_tensor(f"y_scratch{l}", (SLOT_TILES * CAP, D), f32).ap() for l in range(DEPTH)]
    y_prompt = outs[0][0].rearrange("(i p) d -> p i d", p=P)
    y_sample = outs[1].rearrange("b s d -> (b s) d")
    v_state_p = outs[2][0, 0]
    v_state_s = outs[3][0].rearrange("b s d -> (b s) d")
    conv_state_p = outs[4][0, 0]
    conv_state_s = outs[5][0].rearrange("b s d -> (b s) d")

    top = [(nc.sbuf_base + 63) // 64 * 64]

    def at(name, shape, dt, off):
        return nc.alloc_sbuf_tensor_at(name, shape, dt, offset=off)

    def new(name, shape, dt=f32):
        n = 4
        for s in shape[1:]:
            n *= s
        off = top[0]
        top[0] += (n + 31) // 32 * 32
        return at(name, shape, dt, off)

    XCOLS = KT * T + 64
    raw = new("w_raw", [P, 4, UNIT])
    whi = new("w_hi", [P, 4, UNIT], f32r)
    wlo = new("w_lo", [P, 4, UNIT], f32r)
    XT0 = top[0]
    xT = new("xT", [P, XCOLS])
    XH0 = top[0]
    xhi = new("x_hi", [P, XCOLS], f32r)
    xlo = new("x_lo", [P, XCOLS], f32r)
    XH1 = top[0]
    ident = new("ident", [P, P])
    below = new("below", [P, P])
    ones = new("ones", [P, P])
    ones_r = new("ones_r", [P, P], f32r)
    iota = new("iota", [P, P])
    tokid = new("tokid", [P, NT])
    iota_e = new("iota_e", [P, NE])
    eps = new("eps", [P, 1])
    cols = new("cols", [P, 64])
    wst = new("w_spatial", [P, NH, P])
    wss = new("w_spatial_s", [TS, NH, TS])
    bsx = new("b_spatial", [P, NH, P + TS], f32r)
    vstat = new("v_stats", [P, NT, VU, 6])
    mv = new("mean_var", [P, NT, 2])
    rstd = new("rstd", [P, NT])
    nmr = new("neg_mean_rstd", [P, NT])
    idx = new("slot_token", [P, SLOT_TILES], u32)
    pos_u = new("token_slot", [P, NT, 2], u32)
    wtop = new("top_weights", [P, 2, NT])
    n_ovf = new("n_overflow", [1, 1], i32)
    ovf_e = new("overflow_expert", [1, OVF], i32)
    S0 = top[0]

    C_BU, C_BG, C_CW = 0, 24, 40
    xtok = at("x_tok", [P, NT, D], f32, S0)
    colsrc = at("cols_src", [64, P], f32, S0 + 20480)
    wsrc = at("w_spatial_src", [P, NH, P], f32, S0 + 20992)
    bsrc = at("b_spatial_src", [1, NH, P], f32, S0 + 23040)
    bss = at("b_spatial_all", [1, NH, P + TS], f32, S0 + 25088)
    bsl = at("b_spatial_low", [1, NH, P + TS], f32r, S0 + 28160)
    vst = at("v_stage", [P, 2, NT, 256], f32, S0)
    bvb = at("v_bias", [P, AW], f32, S0 + 31232)
    ghi = at("g_hi", [P, ROUND, T], f32r, S0)
    glo = at("g_lo", [P, ROUND, T], f32r, S0 + 9216)
    gf = at("g_full", [P, 2, T], f32, S0 + 18432)
    vc = at("v_cols", [P, NT, 512], f32, S0 + 23040)
    gb = at("v_ln", [P, 2, 512], f32, S0 + 33280)
    conv = at("conv", [P, KT, T], f32, S0 + 23200)
    HP = 2 + TP + RB * (2 + SB)
    cx = at("conv_in", [P, 2, HP], f32, S0 + 18432)
    c_sb = at("c_gate", [P, 2, T], f32, S0)
    past = at("past_src", [RB * 2, D], f32, S0 + 4608)
    pastT = at("pastT", [P, KT, RB * 2], f32, S0 + 8704)
    last = at("conv_last", [P, KT, 2 + 2 * RB], f32, S0 + 41632)
    last_o = at("conv_last_rows", [2 + 2 * RB, D], f32, S0 + 42208)
    ppT = at("ple_projT", [P, KT, T], f32, S0 + 20480)
    sgm = at("ple_gate", [P, 2, T], f32, S0)
    o_sb = at("y_rows", [P, 2, D], f32, S0)

    def xh(name, shape, dt, off):
        n = 4
        for s in shape[1:]:
            n *= s
        assert XH0 + off + n <= XH1, name
        return at(name, shape, dt, XH0 + off)

    lnp = xh("ln_params", [P, 2, D], f32, 0)
    p_tok = xh("p_tok", [P, NT, PLE], f32, 8192)
    pThi = xh("pT_hi", [P, 2, T], f32r, 13312)
    pTlo = xh("pT_lo", [P, 2, T], f32r, 17920)
    x1T = xh("x1T", [P, KT, P], f32, 22528)
    wr = xh("w_router", [P, KT, 20], f32, 26624)
    br = xh("b_router", [P, 20], f32, 27264)
    rt = xh("routing", [P, 1120], f32, 27648)
    roff = [0]

    def rtile(*shape):
        n = 1
        for s in shape:
            n *= s
        a = rt[:, roff[0]:roff[0] + n]
        roff[0] += n
        if len(shape) == 2:
            a = a.rearrange("p (a b) -> p a b", b=shape[1])
        if len(shape) == 3:
            a = a.rearrange("p (a b c) -> p a b c", b=shape[1], c=shape[2])
        return a

    lg = rtile(NT, 20)
    r4 = rtile(NT, 4)
    ohg = rtile(NT, 4)
    oh1 = rtile(NT, 4)
    oh2 = rtile(NT, 4)
    ein = rtile(NT, 4)
    s5 = rtile(8, NT)
    m16 = rtile(NT, NE)
    oh16 = [rtile(NT, 4, 4), rtile(NT, 4, 4)]
    t16 = rtile(NT, 4, 4)
    post = rtile(NT, NE)
    ovw = rtile(6, 24)
    wide = rtile(OVF, NE)
    pmd = rtile(3, 2 * NT)
    amat = xh("slot_onehot", [P, 2, P], f32, 32512)
    bmat = xh("tile_onehot", [P, 2, SLOT_TILES], f32, 33536)
    posi = xh("pos_int", [P, 3, 2 * NT], i32, 33728)
    xg = xh("x_gathered", [P, 2, D], f32, 0)
    eTh = xh("xgT_hi", [P, D], f32r, 8192)
    eTl = xh("xgT_lo", [P, D], f32r, 12288)
    act_a = xh("expert_act", [P, 2, F], f32, 16384)
    aTh = xh("expert_actT_hi", [P, F], f32r, 18432)
    aTl = xh("expert_actT_lo", [P, F], f32r, 19456)
    y_sb = xh("expert_y", [P, D], f32, 20480)
    eTf = xh("xgT_full", [P, D], f32, 24576)
    aTf = xh("expert_actT_full", [P, F], f32, 28672)
    yg = xh("y_gathered", [P, 2, 2, D], f32, 8192)

    ctx = ExitStack()
    with ctx:
        ps = ctx.enter_context(nc.psum_tensor("ps", [P, 8, 512], f32))

        def sem(name):
            return ctx.enter_context(nc.semaphore(name))

        wld = [sem(f"w_loaded{j}") for j in range(4)]
        x_ld, small_ld, ws_ld, bv_ld = sem("x_loaded"), sem("small_loaded"), sem("ws_loaded"), sem("v_bias_loaded")
        blk_ld, bsl_ld = sem("blocks_loaded"), sem("bias_low_loaded")
        vc_ld, ln_ld, p_ld, wr_ld, past_ld = sem("v_cols_loaded"), sem("ln_loaded"), sem("p_loaded"), sem("router_loaded"), sem("past_loaded")
        xg_ld = [sem("x_gathered0"), sem("x_gathered1")]
        yg_ld = [sem("y_gathered0"), sem("y_gathered1")]
        ov_ld, ovx_ld = [sem("ovf_w0"), sem("ovf_w1")], [sem("ovf_x0"), sem("ovf_x1")]
        hi_done, split_done = sem("w_hi_done"), sem("w_split_done")
        eu_used = sem("expert_unit_used")
        mt_done = sem("pair_done")
        const_ok, cols_ok, ws_t, ws_cp, ws_ok = sem("consts_ready"), sem("cols_ready"), sem("ws_turned"), sem("ws_copied"), sem("ws_ready")
        bs_ok, bsh_ok, bsl_ok, ones_ok = sem("bias_spread"), sem("bias_high"), sem("bias_low"), sem("ones_ready")
        tr_done, tr_free = sem("turned"), sem("turned_free")
        xT_ok, xhi_ok, xlo_ok = sem("xT_ready"), sem("xhi_ready"), sem("xlo_ready")
        vps_done, vz_done, vg_done, vs_done, v_st = sem("v_product"), sem("v_biased"), sem("v_gelu"), sem("v_stats_done"), [sem("v_stored0"), sem("v_stored1")]
        vn_ok, vstate_st, sg_done, gm_done = sem("v_normed"), sem("v_state_stored"), sem("gate_product"), sem("g_done")
        u_done, gh_done, gl_done = sem("u_done"), sem("g_hi_done"), sem("g_lo_done")
        o_done = sem("out_added")
        pp_done = sem("ple_proj_copied")
        st_ok, sq_ok, rs_ok, nz_ok, ng_ok, nb_ok = sem("stats_ready"), sem("std_ready"), sem("rstd_ready"), sem("normed"), sem("norm_scaled"), sem("norm_done")
        x_st = sem("x_stored")
        p_turn, ph_ok, pl_ok = sem("p_turned"), sem("pT_hi_ready"), sem("pT_lo_ready")
        r_turn, r_cp, r_mm, r_lg = sem("router_turned"), sem("router_copied"), sem("router_product"), sem("logits_ready")
        r_ex, r_ex_ok, m_ok, rank_ok, ab_ok, ab_used, idx_ok = sem("exp_asked"), sem("exp_ready"), sem("onehot_ready"), sem("rank_ready"), sem("slot_onehot_ready"), sem("slot_onehot_used"), sem("idx_ready")
        xs_ok = sem("x_scaled")
        xtp, eth_ok, etl_ok = sem("xg_turned"), sem("xgT_hi_ready"), sem("xgT_lo_ready")
        si_ok, a_ok, at_ok, ath_ok, atl_ok = sem("silu_done"), sem("a_ready"), sem("a_turned"), sem("aT_hi_ready"), sem("aT_lo_ready")
        y_cp, y_st = sem("y_copied"), sem("y_stored")
        ov = [{n: sem(f"ovf_{n}{l}") for n in ("turned", "copied", "gu", "silu", "a", "aturned", "acopied", "y", "ycopied", "stored")} for l in range(DEPTH)]
        sg_ok, pe_ok = sem("gate_ready"), sem("layer_done")
        c_ok, cx_ok = sem("c_copied"), sem("cx_ready")
        past_t, past_ok, last_ok, last_t, last_cp, cs_st = sem("past_turned"), sem("past_ready"), sem("last_ready"), sem("last_turned"), sem("last_copied"), sem("conv_state_stored")
        out_cp, out_st = sem("rows_copied"), [sem("rows_stored0"), sem("rows_stored1")]
        dch, ach, pch = sem("vector_chain"), sem("scalar_chain"), sem("pool_chain")

        block = ctx.enter_context(nc.Block())

        def tok(i):
            return P if i < NT - 1 else TS

        def w8(w, j, k, c0, n=P):
            return w[:, j, k * 256 + c0:k * 256 + c0 + n]

        def w4(w, j, k, c0, n=P):
            return w[:, j, k * 512 + c0:k * 512 + c0 + n]

        def xk(x, k, c0, n):
            return x[:, k * T + c0:k * T + c0 + n]

        def pair(par):
            return ps[:, 2 * par:2 * par + 2, 0:HALF]

        def halves(a):
            return a.rearrange("p (h t) -> p h t", h=2)

        def turned_bank(n):
            return 4 + 2 * (n % 2)

        def loads_of_slot(d):
            return 16 * (d // 4 + 1)

        def gu_unit(s):
            return 3 * s - 1 if s else 0

        def dn_unit(s):
            return 3 * s + 4 if s < NE - 1 else EU - 1

        def tiles_through(d):
            if d < U_P[0]:
                r, j = divmod(d - U_A, 4)
                return M_A + 12 * r + (2, 4, 8, 12)[j]
            if U_B <= d < U_P[1]:
                r, j = divmod(d - U_B, 4)
                return M_B + 12 * r + (2, 4, 8, 12)[j]
            for u0, m0 in ((U_G[1], M_G[1]), (U_P[1], M_P[1]), (U_CH, M_CH), (U_G[0], M_G[0]), (U_P[0], M_P[0])):
                if d >= u0:
                    return m0 + 2 * (d - u0 + 1)

        def wait_used(eng, d, it=0, step=0):
            for l in range(DEPTH):
                if U_E[l] + 4 <= d < U_G[l] + 4:
                    eng.wait_ge(eu_used, it * step + (EU * l + d - U_E[l] - 3))
                    return
            if d - 4 >= U_A:
                eng.wait_ge(mt_done, it * (3 * step) + tiles_through(d - 4))
            elif d >= 4:
                eng.wait_ge(vps_done, it * (NT * step) + NT * (d - 3))

        TR_IN = 0
        TR_N1 = [NT, NT * 4]
        TR_RT = [NT * 2, NT * 5]
        TR_N2 = [NT * 3, NT * 6]
        TR_OUT = NT * 7
        TF_RT = [NT, NT * 3]
        TF_N2 = [NT * 2, NT * 4]
        V_DONE = NT * VU

        @block.sync
        def _(sp):
            nc.allow_non_contiguous_dma(reason="rows of weight units")

            def load_unit(d, j, src, n=UNIT, shape=None, it=None, wait=None):
                if wait is not None:
                    sp.wait_ge(split_done, wait)
                sp.dma_start(raw[:, j, 0:n] if shape is None else raw[:, j, 0:n].rearrange("p (k c) -> p k c", c=shape),
                             src).then_inc(wld[j], 16)

            def cols8(w, c0):
                return w[:, ds(c0, 256)].rearrange("(k p) c -> p k c", p=P)

            def rows4(w, r0, c0):
                return w[ds(r0, 512), c0:c0 + 512].rearrange("(k p) c -> p k c", p=P)

            sp.dma_start(xtok[:, 0:4, :], x_prompt).then_inc(x_ld, 16)
            sp.dma_start(xtok[0:TS, 4, :], x_sample).then_inc(x_ld, 16)
            for j in range(4):
                load_unit(j, j, cols8(w_in, AW + 256 * j), shape=256)
            with sp.Fori(1, VU // 4) as it:
                for j in range(4):
                    load_unit(0, j, cols8(w_in, it * 1024 + (AW + 256 * j)), shape=256, wait=it * 4 + (U_V + j - 3))
            with sp.Fori(0, AR) as it:
                for j in range(2):
                    load_unit(0, j, cols8(w_in, it * 512 + 256 * j), shape=256, wait=it * 4 + (U_A + j - 3))
                for j in range(2):
                    load_unit(0, 2 + j, rows4(w_out, it * 512, 512 * j), shape=512, wait=it * 4 + (U_A + 2 + j - 3))
            for l in range(DEPTH):
                for j in range(4):
                    load_unit(0, j, x_in["ple_w_proj"][l][:, 256 * j:256 * j + 256].rearrange("(k p) c -> p k c", p=P),
                              n=512, shape=256, wait=U_P[l] + j - 3)
                g_src, d_src = x_in["moe_w_gate_up"][l], x_in["moe_w_down"][l]

                def expert_load(e, src, width, it=None):
                    d = U_E[l] + e
                    sp.wait_ge(split_done, d - 3 if it is None else it * 12 + (d - 3))
                    sp.dma_start(raw[:, e % 4, :].rearrange("p (k c) -> p k c", c=width), src).then_inc(wld[e % 4], 16)

                def load_step(s, it=None):
                    at_ = s if it is None else it * 4 + s
                    if s < NE:
                        for a in range(2):
                            expert_load(gu_unit(s) + a, g_src[at_, 512 * a:512 * a + 512, :].rearrange("(k p) c -> p k c", p=P), 2 * F, it)
                    if s:
                        expert_load(dn_unit(s - 1), d_src[at_ - 1, :, :].rearrange("(k p) c -> p k c", p=P), D, it)

                load_step(0)
                load_step(1)
                with sp.Fori(0, 3) as it:
                    for s in range(2, 6):
                        load_step(s, it)
                for s in range(NE - 2, NE + 1):
                    load_step(s)
                sp.wait_ge(idx_ok, 3 * (l + 1))
                n = sp.value_load(n_ovf[0:1, 0:1], min_val=0, max_val=OVF)
                with sp.If(n > 0):
                    sp.wait_ge(split_done, U_G[l])

                    def ovf_load(i):
                        e = sp.value_load(ovf_e[0:1, ds(i, 1)], min_val=0, max_val=NE - 1)
                        for a in range(2):
                            sp.dma_start(raw[:, a, :].rearrange("p (k c) -> p k c", c=2 * F),
                                         g_src[ds(e, 1), 512 * a:512 * a + 512, :].rearrange("e (k p) c -> p (e k) c", p=P)).then_inc(ov_ld[l], 16)
                        sp.dma_start(raw[:, 2, :].rearrange("p (k c) -> p k c", c=D),
                                     d_src[ds(e, 1), :, :].rearrange("e (k p) c -> p (e k) c", p=P)).then_inc(ov_ld[l], 16)

                    ovf_load(0)
                    with sp.Fori(1, OVF) as i:
                        sp.wait_ge(ov[l]["y"], i)
                        ovf_load(i)
                    sp.wait_ge(ov[l]["y"], OVF)
                for j in range(4):
                    load_unit(0, j, cols8(x_in["ple_w_gate"][l], 256 * j), shape=256, wait=U_G[l] + j - 3)
                if l == 0:
                    with sp.Fori(0, 2) as it:
                        for j in range(4):
                            load_unit(0, j, cols8(bw_in, it * 512 + (D * (1 + j % 2) + 256 * (j // 2))), shape=256,
                                      wait=it * 4 + (U_CH + j - 3))
                    with sp.Fori(0, BR) as it:
                        for j in range(2):
                            load_unit(0, j, cols8(bw_in, it * 512 + 256 * j), shape=256, wait=it * 4 + (U_B + j - 3))
                        for j in range(2):
                            load_unit(0, 2 + j, rows4(bw_out, it * 512, 512 * j), shape=512, wait=it * 4 + (U_B + 2 + j - 3))
            for i in range(NT):
                sp.wait_ge(out_cp, i + 1)
                dst = y_prompt[:, i, :] if i < 4 else y_sample
                sp.dma_start(dst, o_sb[0:tok(i), i % 2, :]).then_inc(out_st[i % 2], 16)
            sp.wait_ge(out_st[0], 48)
            sp.wait_ge(out_st[1], 32)

        @block.gpsimd
        def _(pool):
            ch = Chain(pool, pch)
            pool.dma_start(colsrc[0:24, :], x_in["a_b_in"][0, 0:AW].rearrange("(f p) -> f p", p=P)).then_inc(small_ld, 16)
            pool.dma_start(colsrc[24:40, :], x_in["ple_b_gate"].rearrange("l (f p) -> (l f) p", p=P)).then_inc(small_ld, 16)
            pool.dma_start(colsrc[40:64, :], x_in["b_conv_w"][0].rearrange("w (f p) -> (w f) p", p=P)).then_inc(small_ld, 16)
            pool.dma_start(wsrc[:, :, :], x_in["a_w_s"][0].rearrange("h t s -> t h s")).then_inc(ws_ld, 16)
            pool.dma_start(bsrc[:, :, :], x_in["a_b_s"]).then_inc(ws_ld, 16)
            pool.dma_start(bvb[:, :], x_in["a_b_in"][0:1, AW:2 * AW].to_broadcast([P, AW])).then_inc(bv_ld, 16)
            ch.link(pool.memset(ident[:, :], 0.0))
            pool.memset(ones[:, :], 1.0)
            pool.memset(below[:, :], 1.0)
            pool.memset(eps[:, :], EPS)
            ch.link(pool.memset(xT[:, KT * T:], 0.0))
            ch.link(pool.memset(xtok[TS:P, 4, :], 0.0))
            ch.link(pool.memset(wss[:, :, :], 0.0))
            pool.affine_select(out=ident[:, :], in_=ident[:, :], compare_op=ALU.not_equal, fill=1.0, base=0,
                               pattern=[[-1, P]], channel_multiplier=1)
            pool.affine_select(out=below[:, :], in_=below[:, :], compare_op=ALU.is_gt, fill=0.0, base=0,
                               pattern=[[1, P]], channel_multiplier=-1)
            pool.iota(iota[:, :], pattern=[[1, P]], base=0, channel_multiplier=0, allow_small_or_imprecise_dtypes=True)
            pool.iota(iota_e[:, :], pattern=[[P, NE]], base=0, channel_multiplier=0, allow_small_or_imprecise_dtypes=True)
            ch.link(pool.iota(tokid[:, :], pattern=[[P, NT]], base=0, channel_multiplier=1, allow_small_or_imprecise_dtypes=True))
            pool.memset(tokid[TS:P, 4:5], 0.0).then_inc(const_ok, 1)
            pool.wait_ge(ws_cp, 1)
            pool.affine_select(out=wst[:, :, :], in_=wst[:, :, :], compare_op=ALU.is_ge, fill=0.0, base=0,
                               pattern=[[0, NH], [1, P]], channel_multiplier=-1).then_inc(ws_ok, 1)
            pool.wait_ge(ws_ok, 1)
            for b in range(RB):
                pool.dma_start(wss[SB * b:SB * b + SB, :, SB * b:SB * b + SB], wst[0:SB, :, 0:SB]).then_inc(blk_ld, 16)
            pool.wait_ge(bsl_ok, 1)
            pool.dma_start(bsx[1:2, :, :], bsl[:, :, :]).then_inc(bsl_ld, 16)
            with pool.Fori(0, VU // 2) as it:
                for j in range(2):
                    pool.wait_ge(vg_done, it * (2 * NT) + NT * (j + 1))
                    dst = v_dram[:, :, ds(it * 512 + 256 * j, 256)]
                    pool.dma_start(dst[0:4].rearrange("i p c -> p i c"), vst[:, j, 0:4, :]).then_inc(v_st[j], 16)
                    pool.dma_start(dst[4, 0:TS, :], vst[0:TS, j, 4, :]).then_inc(v_st[j], 16)
            pool.wait_ge(v_st[0], VU // 2 * 32)
            pool.wait_ge(v_st[1], VU // 2 * 32)

            def vcols(r):
                pool.dma_start(vc[:, 0:4, :], v_dram[0:4, :, ds(r * 512, 512)].rearrange("i p c -> p i c")).then_inc(vc_ld, 16)
                pool.dma_start(vc[0:TS, 4, :], v_dram[4, 0:TS, ds(r * 512, 512)]).then_inc(vc_ld, 16)
                for n, name in enumerate(("a_ln_g", "a_ln_b")):
                    pool.dma_start(gb[:, n, :], x_in[name][0:1, ds(r * 512, 512)].to_broadcast([P, 512])).then_inc(vc_ld, 16)

            def vstate(r):
                pool.dma_start(v_state_p[:, ds(r * 512, 512)], vc[:, 3, :]).then_inc(vstate_st, 16)
                pool.dma_start(v_state_s[:, ds(r * 512, 512)], vc[0:TS, 4, :]).then_inc(vstate_st, 16)

            pool.wait_ge(xlo_ok, NT)
            vcols(0)
            with pool.Fori(0, AR - 1) as r:
                pool.wait_ge(vn_ok, r * NT + NT)
                vstate(r)
                pool.wait_ge(vstate_st, r * 32 + 32)
                pool.wait_ge(sg_done, r * ROUND + ROUND)
                vcols(r + 1)
            pool.wait_ge(vn_ok, AR * NT)
            vstate(AR - 1)
            pool.wait_ge(vstate_st, AR * 32)

            def ln_load(g, b):
                pool.dma_start(lnp[:, 0, :], g.to_broadcast([P, D])).then_inc(ln_ld, 16)
                pool.dma_start(lnp[:, 1, :], b.to_broadcast([P, D])).then_inc(ln_ld, 16)

            for l in range(DEPTH):
                pool.wait_ge(mt_done, M_P[l] - KT)
                ln_load(x_in["ln1_g"][l:l + 1, :], x_in["ln1_b"][l:l + 1, :])
                pool.dma_start(p_tok[:, 0:4, :], x_in["p_prompt"][l, 0].rearrange("(i p) d -> p i d", p=P)).then_inc(p_ld, 16)
                pool.dma_start(p_tok[0:TS, 4, :], x_in["p_sample"][l].rearrange("b s d -> (b s) d")).then_inc(p_ld, 16)
                pool.dma_start(wr[:, :, 0:4], x_in["moe_w_group"][l].rearrange("(k p) c -> p k c", p=P)).then_inc(wr_ld, 16)
                pool.dma_start(wr[:, :, 4:20], x_in["moe_w_expert"][l].rearrange("(k p) c -> p k c", p=P)).then_inc(wr_ld, 16)
                pool.dma_start(br[:, 0:4], x_in["moe_b_group"][l:l + 1, :].to_broadcast([P, 4])).then_inc(wr_ld, 16)
                pool.dma_start(br[:, 4:20], x_in["moe_b_expert"][l:l + 1, :].to_broadcast([P, 16])).then_inc(wr_ld, 16)
                for i in range(NT):
                    pool.wait_ge(ng_ok, 2 * NT * l + i + 1)
                    pool.tensor_tensor(xtok[:, i, :], xtok[:, i, :], lnp[:, 1, :], ALU.add).then_inc(nb_ok, 1)
                    pool.wait_ge(nb_ok, 2 * NT * l + i + 1)
                    pool.dma_start(x_dram[l][P * i:P * i + tok(i), :], xtok[0:tok(i), i, :]).then_inc(x_st, 16)
                pool.wait_ge(x_st, 16 * NT * (l + 1))
                pool.wait_ge(idx_ok, 3 * (l + 1))

                def gather(s):
                    if s >= 2:
                        pool.wait_ge(xtp, 2 * (NE * l + s - 1))
                    pool.indirect_dma_start(out=xg[:, s % 2, :], out_offset=None, in_=x_dram[l][:, :],
                                            in_offset=bass.IndirectOffsetOnAxis(ap=idx[:, s:s + 1], axis=0)).then_inc(xg_ld[s % 2], 16)

                for s in range(NE):
                    gather(s)
                n = pool.value_load(n_ovf[0:1, 0:1], min_val=0, max_val=OVF)
                with pool.If(n > 0):
                    o = ov[l]
                    pool.wait_ge(xtp, 2 * NE * (l + 1))
                    for i in range(OVF):
                        if i:
                            pool.wait_ge(o["turned"], i)
                        pool.indirect_dma_start(out=xg[:, 0, :], out_offset=None, in_=x_dram[l][:, :],
                                                in_offset=bass.IndirectOffsetOnAxis(ap=idx[:, NE + i:NE + i + 1], axis=0)).then_inc(ovx_ld[l], 16)
                    pool.wait_ge(o["stored"], 16 * OVF)
                pool.wait_ge(y_st, 16 * NE * (l + 1))
                pool.wait_ge(etl_ok, 2 * NE * (l + 1))
                pool.wait_ge(eu_used, EU * (l + 1))
                ln_load(x_in["ln2_g"][l:l + 1, :], x_in["ln2_b"][l:l + 1, :])

                def norm2(rows):
                    for i in range(NT + 2):
                        if i < NT:
                            if i >= 2:
                                pool.wait_ge(st_ok, 2 * NT * l + NT + i - 1)
                            for k in range(2):
                                pool.indirect_dma_start(out=yg[0:tok(i), i % 2, k, :], out_offset=None, in_=y_dram[l][0:rows, :],
                                                        in_offset=bass.IndirectOffsetOnAxis(ap=pos_u[0:tok(i), i, k:k + 1], axis=0)).then_inc(yg_ld[i % 2], 16)
                        if i >= 2:
                            pool.wait_ge(ng_ok, 2 * NT * l + NT + i - 1)
                            pool.tensor_tensor(xtok[:, i - 2, :], xtok[:, i - 2, :], lnp[:, 1, :], ALU.add).then_inc(nb_ok, 1)

                with pool.If(n > 0):
                    norm2(SLOT_TILES * CAP)
                with pool.If(n < 1):
                    norm2(NE * CAP)
                if l == 0:
                    pool.wait_ge(pe_ok, KT)
                    pool.dma_start(past[:, :], x_in["state_conv"][0].rearrange("b w d -> (b w) d")).then_inc(past_ld, 16)
                    pool.wait_ge(last_cp, 1)
                    pool.dma_start(conv_state_p, last_o[0:2, :]).then_inc(cs_st, 16)
                    pool.dma_start(conv_state_s, last_o[2:18, :]).then_inc(cs_st, 16)
                    pool.wait_ge(cs_st, 32)

        @block.scalar
        def _(act):
            ch = Chain(act, ach)

            def hi(d, it=0, step=0):
                j = d % 4
                n = 512 if U_P[0] <= d < U_E[0] or U_P[1] <= d < U_E[1] else UNIT
                assert step % 4 == 0
                act.wait_ge(wld[j], it * (4 * step) + loads_of_slot(d))
                wait_used(act, d, it, step)
                act.activation(whi[:, j, 0:n], raw[:, j, 0:n], ACT.Copy).then_inc(hi_done, 1)

            for i in range(NT):
                act.wait_ge(tr_done, TR_IN + i + 1)
                b = turned_bank(TR_IN + i)
                src = ps[:, b:b + 2, :].rearrange("p b (k t) -> p (b k) t", t=P)[:, :, 0:tok(i)]
                dst = xT[:, 0:KT * T].rearrange("p (k t) -> p k t", t=T)[:, :, P * i:P * i + tok(i)]
                act.activation(dst, src, ACT.Copy).then_inc(tr_free, 1)
                act.wait_ge(tr_free, TR_IN + i + 1)
                act.activation(xhi[:, 0:KT * T].rearrange("p (k t) -> p k t", t=T)[:, :, P * i:P * i + tok(i)], dst,
                               ACT.Copy).then_inc(xhi_ok, 1)
                if i < 4:
                    hi(i)
            act.activation(xhi[:, KT * T:], xT[:, KT * T:], ACT.Copy).then_inc(xhi_ok, 1)
            act.wait_ge(bs_ok, 1)
            act.activation(bsx[0:1, :, :], bss[:, :, :], ACT.Copy).then_inc(bsh_ok, 1)
            act.wait_ge(const_ok, 1)
            act.activation(ones_r[:, :], ones[:, :], ACT.Copy).then_inc(ones_ok, 1)

            def v_unit(n, it=0, step=0):
                for i in range(NT):
                    act.wait_ge(vz_done, it * (NT * step) + (NT * n + i + 1))
                    act.activation(vst[:, n % 2, i, :], vst[:, n % 2, i, :], ACT.Gelu).then_inc(vg_done, 1)
                    if i == 1 and n + AHEAD >= 4:
                        hi(n + AHEAD, it, step)

            for n in range(2):
                v_unit(n)
            with act.Fori(0, (VU - 4) // 4) as it:
                for j in range(4):
                    v_unit(2 + j, it, 4)
            for n in (VU - 2, VU - 1):
                v_unit(n)
            act.wait_ge(rs_ok, 1)
            act.activation(rstd[:, :], rstd[:, :], ACT.Sqrt).then_inc(sq_ok, 1)

            def a_round(r, it, step, split):
                for fl in range(ROUND):
                    act.wait_ge(gl_done, it * (ROUND * step) + (ROUND * r + fl - 1)) if (r or step or fl >= 2) else None
                    act.wait_ge(mt_done, it * (12 * step) + (M_A + 12 * r + fl + 1))
                    act.wait_ge(cols_ok, 1)
                    act.activation(halves(gf[:, fl % 2, :]), pair(fl % 2), ACT.Gelu,
                                   bias=cols[:, ds(it * (ROUND * step) + (C_BU + ROUND * r + fl), 1)]).then_inc(u_done, 1)
                    if fl % 2 == 0:
                        split(fl // 2)
                    act.wait_ge(gm_done, it * (ROUND * step) + (ROUND * r + fl + 1))
                    act.activation(ghi[:, fl, :], gf[:, fl % 2, :], ACT.Copy).then_inc(gh_done, 1)
                split(2)
                split(3)

            a_round(0, 0, 0, lambda j: hi(U_A + j + AHEAD))
            with act.Fori(0, AR - 2) as it:
                a_round(1, it, 1, lambda j: hi(U_A + 4 + j + AHEAD, it, 4))
            a_round(AR - 1, 0, 0, lambda j: hi(U_P[0] - 4 + j + AHEAD))

            def norm_tile(l, which, i):
                n = 2 * NT * l + NT * which + i
                act.wait_ge(st_ok, n + 1)
                act.activation(rstd[:, i:i + 1], mv[:, i, 1:2], ACT.Sqrt, bias=eps[:, 0:1]).then_inc(sq_ok, 1)
                act.wait_ge(rs_ok, 1 + n + 1)
                if which == 0:
                    b = turned_bank(TR_N1[l] + i)
                    dst, src = xtok[:, i, :].rearrange("p (b t) -> p b t", b=2), ps[:, b:b + 2, :]
                else:
                    dst, src = xtok[:, i, :], xtok[:, i, :]
                act.activation(dst, src, ACT.Identity, bias=nmr[:, i:i + 1], scale=rstd[:, i:i + 1]).then_inc(nz_ok, 1)

            for l in range(DEPTH):
                norm_tile(l, 0, 0)
                norm_tile(l, 0, 1)
                for i in range(NT):
                    act.wait_ge(p_turn, NT * l + i + 1)
                    act.activation(pThi[:, :, P * i:P * i + tok(i)],
                                   ps[:, i % 4, 0:2 * P].rearrange("p (k t) -> p k t", t=P)[:, :, 0:tok(i)], ACT.Copy).then_inc(ph_ok, 1)
                hi(U_P[l] + AHEAD)
                for i in range(2, NT):
                    norm_tile(l, 0, i)

                def proj_out(mo):
                    act.wait_ge(mt_done, M_P[l] + mo + 1)
                    act.activation(halves(ppT[:, mo, :]), pair(mo % 2), ACT.Copy).then_inc(pp_done, 1)

                for mo in range(4):
                    proj_out(mo)
                for i in range(NT):
                    b = turned_bank(TR_RT[l] + i)
                    act.wait_ge(tr_done, TR_RT[l] + i + 1)
                    if i:
                        act.wait_ge(r_mm, NT * l + i)
                    act.activation(x1T[:, :, :].rearrange("p (b k) t -> p b (k t)", b=2), ps[:, b:b + 2, :],
                                   ACT.Copy).then_inc(tr_free, 1)
                proj_out(4)
                proj_out(5)
                act.wait_ge(r_ex, 2 * l + 1)
                act.activation(r4[:, :, :], r4[:, :, :], ACT.Exp).then_inc(r_ex_ok, 1)
                act.wait_ge(r_ex, 2 * l + 2)
                act.activation(s5[:, 3, :], s5[:, 3, :], ACT.Exp).then_inc(r_ex_ok, 1)
                proj_out(6)
                proj_out(7)

                def xT_hi(s, it=0, step=0):
                    q = it * (2 * step) + 2 * (NE * l + s)
                    for b in range(2):
                        act.wait_ge(xtp, q + (b + 1))
                        act.activation(eTh[:, 512 * b:512 * b + 512], ps[:, 2 + b, :], ACT.Copy).then_inc(eth_ok, 1)

                def y_out(s, it=0, step=0):
                    q = it * step + (NE * l + s)
                    act.wait_ge(eu_used, it * (3 * step) + (EU * l + dn_unit(s) + 1))
                    if l or s or step:
                        act.wait_ge(y_st, q * 16)
                    act.activation(y_sb[:, :].rearrange("p (b t) -> p b t", b=2), ps[:, 4:6, :], ACT.Copy).then_inc(y_cp, 1)
                    act.wait_ge(y_cp, q + 1)
                    act.dma_start(y_dram[l][ds(it * (P * step) + P * s, P), :], y_sb[:, :]).then_inc(y_st, 16)

                def expert_hi(e, it, step):
                    if e < EU:
                        hi(U_E[l] + e, it, 3 * step)

                def moe_step(s, it=0, step=0):
                    e = 3 * s + 2
                    expert_hi(e, it, step)
                    expert_hi(e + 1, it, step)
                    if s < NE:
                        q = it * step + (NE * l + s)
                        act.wait_ge(eu_used, it * (3 * step) + (EU * l + gu_unit(s) + 2))
                        act.activation(act_a[:, 0, :], ps[:, 0, 0:F], ACT.Silu).then_inc(si_ok, 1)
                    if s < NE - 1:
                        xT_hi(s + 1, it, step)
                        expert_hi(e + 2, it, step)
                    if s >= 1:
                        y_out(s - 1, it, step)
                    if s < NE:
                        act.wait_ge(at_ok, q + 1)
                        act.activation(aTh[:, :], ps[:, 1, 0:F], ACT.Copy).then_inc(ath_ok, 1)

                hi(U_E[l])
                hi(U_E[l] + 1)
                act.wait_ge(x_st, 16 * NT * (l + 1))
                act.activation(xtok[:, :, :], xtok[:, :, :], ACT.Copy, scale=ALPHA).then_inc(xs_ok, 1)
                xT_hi(0)
                moe_step(0)
                moe_step(1)
                with act.Fori(0, 3) as it:
                    for s in range(2, 6):
                        moe_step(s, it, 4)
                for s in range(NE - 2, NE + 1):
                    moe_step(s)
                act.wait_ge(idx_ok, 3 * (l + 1))
                n = act.value_load(n_ovf[0:1, 0:1], min_val=0, max_val=OVF)
                with act.If(n > 0):
                    o = ov[l]
                    act.wait_ge(y_st, 16 * NE * (l + 1))
                    with act.Fori(0, OVF) as i:
                        act.wait_ge(o["turned"], i + 1)
                        act.activation(eTf[:, :].rearrange("p (b t) -> p b t", b=2), ps[:, 2:4, :], ACT.Copy).then_inc(o["copied"], 1)
                        act.wait_ge(o["gu"], i + 1)
                        act.activation(act_a[:, 0, :], ps[:, 0, 0:F], ACT.Silu).then_inc(o["silu"], 1)
                        act.wait_ge(o["aturned"], i + 1)
                        act.activation(aTf[:, :], ps[:, 1, 0:F], ACT.Copy).then_inc(o["acopied"], 1)
                        act.wait_ge(o["y"], i + 1)
                        act.activation(y_sb[:, :].rearrange("p (b t) -> p b t", b=2), ps[:, 4:6, :], ACT.Copy).then_inc(o["ycopied"], 1)
                        act.wait_ge(o["ycopied"], i + 1)
                        act.dma_start(y_dram[l][ds(i * P + NE * P, P), :], y_sb[:, :]).then_inc(o["stored"], 16)
                        act.wait_ge(o["stored"], i * 16 + 16)
                for j in range(AHEAD):
                    hi(U_G[l] + j)
                for i in range(NT):
                    norm_tile(l, 1, i)
                for i in range(NT):
                    b = turned_bank(TR_N2[l] + i)
                    act.wait_ge(tr_done, TR_N2[l] + i + 1)
                    src = ps[:, b:b + 2, :].rearrange("p b (k t) -> p (b k) t", t=P)[:, :, 0:tok(i)]
                    act.activation(xT[:, 0:KT * T].rearrange("p (k t) -> p k t", t=T)[:, :, P * i:P * i + tok(i)], src,
                                   ACT.Copy).then_inc(tr_free, 1)

                def x_hi(wait_sem, value):
                    act.wait_ge(wait_sem, value)
                    for k in range(KT):
                        act.activation(xk(xhi, k, 0, T), xk(xT, k, 0, T), ACT.Copy).then_inc(xhi_ok, 1)

                x_hi(tr_free, TF_N2[l] + NT)
                for j in range(4):
                    if U_G[l] + j + AHEAD < U_END:
                        hi(U_G[l] + j + AHEAD)
                    for m in range(2):
                        mo = 2 * j + m
                        act.wait_ge(mt_done, M_G[l] + mo + 1)
                        if mo >= 2:
                            act.wait_ge(pe_ok, KT * l + mo - 1)
                        act.activation(halves(sgm[:, m, :]), pair(m), ACT.Sigmoid,
                                       bias=cols[:, C_BG + KT * l + mo:C_BG + KT * l + mo + 1]).then_inc(sg_ok, 1)
                if l == 0:
                    act.wait_ge(mt_done, M_G[0] + KT)
                    x_hi(pe_ok, KT)

                    for jj in range(4):
                        for m in range(2):
                            act.wait_ge(mt_done, M_CH + 4 * jj + m + 1)
                            if jj:
                                act.wait_ge(cx_ok, 2 * jj - 1 + m)
                            act.activation(halves(c_sb[:, m, :]), pair(m), ACT.Copy).then_inc(c_ok, 1)
                        hi(U_CH + 2 * jj + AHEAD)
                        hi(U_CH + 2 * jj + 1 + AHEAD)
                    for r in range(BR):
                        for fl in range(ROUND):
                            q = ROUND * (AR + r) + fl
                            act.wait_ge(gm_done, q + 1)
                            act.activation(ghi[:, fl, :], gf[:, fl % 2, :], ACT.Copy).then_inc(gh_done, 1)
                            hi(U_B + 4 * r + fl + AHEAD)
                        if r == 0:
                            act.wait_ge(last_t, 1)
                            act.activation(last_o[:, :].rearrange("p (b t) -> p b t", b=2), ps[0:18, 6:8, :],
                                           ACT.Copy).then_inc(last_cp, 1)
            for i in range(NT):
                b = turned_bank(TR_OUT + i)
                act.wait_ge(tr_done, TR_OUT + i + 1)
                if i >= 2:
                    act.wait_ge(out_st[i % 2], 16 * (i // 2))
                act.activation(o_sb[:, i % 2, :].rearrange("p (b t) -> p b t", b=2), ps[:, b:b + 2, :],
                               ACT.Copy).then_inc(out_cp, 1)

        @block.vector
        def _(dve):
            ch = Chain(dve, dch)

            def lo(d, it=0, step=0):
                j = d % 4
                n = 512 if U_P[0] <= d < U_E[0] or U_P[1] <= d < U_E[1] else UNIT
                dve.wait_ge(hi_done, it * step + (d + 1))
                dve.tensor_tensor(wlo[:, j, 0:n], raw[:, j, 0:n], whi[:, j, 0:n].bitcast(f32), ALU.subtract).then_inc(split_done, 1)

            for i in range(NT):
                v = [x[:, 0:KT * T].rearrange("p (k t) -> p k t", t=T)[:, :, P * i:P * i + tok(i)] for x in (xlo, xT, xhi)]
                dve.wait_ge(xhi_ok, i + 1)
                dve.tensor_tensor(v[0], v[1], v[2].bitcast(f32), ALU.subtract).then_inc(xlo_ok, 1)
                if i < 4:
                    lo(i)
            dve.wait_ge(xhi_ok, NT + 1)
            dve.tensor_tensor(xlo[:, KT * T:], xT[:, KT * T:], xhi[:, KT * T:].bitcast(f32), ALU.subtract).then_inc(xlo_ok, 1)
            dve.wait_ge(ws_t, 1)
            dve.tensor_copy(cols[:, :], ps[:, 0, 0:64]).then_inc(cols_ok, 1)
            dve.tensor_copy(wst[:, :, :], ps[:, 1, :].rearrange("p (h t) -> p h t", h=NH)).then_inc(ws_cp, 1)
            dve.wait_ge(ws_ld, 32)
            dve.memset(bsx[:, :, :].bitcast(f32), 0.0)
            dve.tensor_copy(bss[:, :, 0:P], bsrc[:, :, :])
            for h in range(NH):
                ins = dve.tensor_copy(bss[:, h, P:].rearrange("o (b t) -> o b t", t=SB),
                                      bsrc[:, h, 0:SB].unsqueeze(1).to_broadcast([1, RB, SB]))
            ins.then_inc(bs_ok, 1)
            dve.wait_ge(bsh_ok, 1)
            dve.tensor_tensor(bsl[:, :, :], bss[:, :, :], bsx[0:1, :, :].bitcast(f32), ALU.subtract).then_inc(bsl_ok, 1)

            def v_stats(n, j, it, step, i):
                dve.wait_ge(vg_done, it * (NT * step) + (NT * n + i + 1))
                dve.bn_stats(vstat[:, i, ds(it * step + n, 1), :].rearrange("p a b -> p (a b)"), vst[:, j % 2, i, :]).then_inc(vs_done, 1)

            def v_unit(n, j, it=0, step=0):
                if n >= 2 or step:
                    dve.wait_ge(v_st[j % 2], it * (16 * step) + (n // 2) * 32)
                for i in range(NT):
                    dve.wait_ge(vps_done, it * (NT * step) + (NT * n + i + 1))
                    dve.tensor_tensor(vst[:, j % 2, i, :], ps[:, (NT * n + i) % 4, 0:256],
                                      bvb[:, ds(it * (256 * step) + 256 * n, 256)], ALU.add).then_inc(vz_done, 1)
                    if i == 2 and n + AHEAD >= 4:
                        lo(n + AHEAD, it, step)
                    if i >= 1:
                        v_stats(n, j, it, step, i - 1)
                v_stats(n, j, it, step, NT - 1)

            dve.wait_ge(bv_ld, 16)
            dve.wait_ge(bsl_ld, 16)
            for j in range(2):
                v_unit(j, j)
            with dve.Fori(0, (VU - 4) // 4) as it:
                for j in range(4):
                    v_unit(2 + j, j, it, 4)
            for n in (VU - 2, VU - 1):
                v_unit(n, n)
            dve.wait_ge(vs_done, NT * VU)
            for i in range(NT):
                ins = dve.bn_aggr(mv[:, i, :], vstat[:, i, :, :].rearrange("p a b -> p (a b)"))
            ch.link(ins)
            dve.tensor_scalar(rstd[:, :], mv[:, :, 1], EPS, None, ALU.add).then_inc(rs_ok, 1)
            dve.wait_ge(sq_ok, 1)
            ch.link(dve.reciprocal(rstd[:, :], rstd[:, :]))
            ch.link(dve.scalar_tensor_tensor(out=nmr[:, :], in0=mv[:, :, 0], scalar=-1.0, in1=rstd[:, :], op0=ALU.mult, op1=ALU.mult))
            ch.link(dve.tensor_scalar(xT[:, :], xT[:, :], ALPHA, None, ALU.mult))

            def v_norm(i):
                t = tok(i)
                ch.link(dve.tensor_scalar(vc[0:t, i, :], vc[0:t, i, :], rstd[0:t, i:i + 1], nmr[0:t, i:i + 1], ALU.mult, ALU.add))
                ch.link(dve.tensor_tensor(vc[0:t, i, :], vc[0:t, i, :], gb[0:t, 0, :], ALU.mult))
                dve.tensor_tensor(vc[0:t, i, :], vc[0:t, i, :], gb[0:t, 1, :], ALU.add).then_inc(vn_ok, 1)

            def gate_product(r, fl, it, step, split):
                q = it * (ROUND * step) + (ROUND * r + fl)
                dve.wait_ge(u_done, q + 1)
                dve.wait_ge(sg_done, q + 1)
                b = 4 + 2 * (fl % 2)
                dve.tensor_tensor(gf[:, fl % 2, 0:TP], gf[:, fl % 2, 0:TP], ps[:, b, :], ALU.mult)
                dve.tensor_tensor(gf[:, fl % 2, TP:T], gf[:, fl % 2, TP:T], ps[:, b + 1, 0:TS], ALU.mult).then_inc(gm_done, 1)
                if fl % 2 == 0:
                    split(fl // 2)
                g_low(q, fl)

            def g_low(q, fl):
                dve.wait_ge(gh_done, q + 1)
                dve.tensor_tensor(glo[:, fl, :], gf[:, fl % 2, :], ghi[:, fl, :].bitcast(f32), ALU.subtract).then_inc(gl_done, 1)

            def add_out(m0, o0, mo, it=0, step=0):
                dve.wait_ge(mt_done, it * (12 * step) + (m0 + 4 + mo + 1))
                if o0 or step:
                    dve.wait_ge(o_done, it * (KT * step) + (o0 - KT + mo + 1))
                x = halves(xk(xT, mo, 0, T))
                dve.tensor_tensor(x, x, pair(mo % 2), ALU.add).then_inc(o_done, 1)

            def a_round(r, it, step, split, norm=True):
                for fl in range(ROUND):
                    gate_product(r, fl, it, step, split)
                for mo in range(KT):
                    if mo == 2:
                        split(2)
                    if mo == 6:
                        split(3)
                    if norm and 2 <= mo < 2 + NT:
                        if mo == 2:
                            dve.wait_ge(vc_ld, it * (64 * step) + 64 * (r + 2))
                        v_norm(mo - 2)
                    add_out(M_A + 12 * r, KT * r, mo, it, step)

            dve.wait_ge(vc_ld, 64)
            for i in range(NT):
                v_norm(i)
            a_round(0, 0, 0, lambda j: lo(U_A + j + AHEAD))
            with dve.Fori(0, AR - 2) as it:
                ch.enter(it, 2 * NT)
                a_round(1, it, 1, lambda j: lo(U_A + 4 + j + AHEAD, it, 4))
            ch.leave(AR - 2)
            a_round(AR - 1, 0, 0, lambda j: lo(U_P[0] - 4 + j + AHEAD), norm=False)

            def rstd_of(i, n):
                dve.wait_ge(sq_ok, 1 + n)
                ch.link(dve.reciprocal(rstd[:, i:i + 1], rstd[:, i:i + 1]))
                dve.scalar_tensor_tensor(out=nmr[:, i:i + 1], in0=mv[:, i, 0:1], scalar=-1.0, in1=rstd[:, i:i + 1],
                                         op0=ALU.mult, op1=ALU.mult).then_inc(rs_ok, 1)

            def scale_of(i, n):
                dve.wait_ge(nz_ok, n)
                dve.tensor_tensor(xtok[:, i, :], xtok[:, i, :], lnp[:, 0, :], ALU.mult).then_inc(ng_ok, 1)

            vs2 = vstat[:, 0, 0:2, :].rearrange("p a b -> p (a b)")

            def first_max(src, oh, mx):
                ch.link(dve.tensor_reduce(out=s5[:, mx, :], in_=src, op=ALU.max, axis=AX.X))
                ch.link(dve.tensor_tensor(oh, src, s5[:, mx, :].unsqueeze(2).to_broadcast([P, NT, 4]), ALU.is_equal))
                ch.link(dve.tensor_tensor(oh, oh, minus4, ALU.mult))
                ch.link(dve.tensor_reduce(out=s5[:, 7, :], in_=oh, op=ALU.min, axis=AX.X))
                ch.link(dve.tensor_tensor(oh, minus4, s5[:, 7, :].unsqueeze(2).to_broadcast([P, NT, 4]), ALU.is_equal))

            for l in range(DEPTH):
                n1 = 2 * NT * l
                dve.wait_ge(ln_ld, 32 * (2 * l + 1))
                if l:
                    dve.wait_ge(vs_done, NT * VU)

                def stats_of(i):
                    dve.wait_ge(tr_done, TR_N1[l] + i + 1)
                    b = turned_bank(TR_N1[l] + i)
                    for h in range(2):
                        ins = dve.bn_stats(vstat[:, i, h, :], ps[:, b + h, :])
                    ch.link(ins)
                    dve.bn_aggr(mv[:, i, :], vstat[:, i, 0:2, :].rearrange("p a b -> p (a b)")).then_inc(st_ok, 1)

                stats_of(0)
                stats_of(1)
                rstd_of(0, n1 + 1)
                rstd_of(1, n1 + 2)
                scale_of(0, n1 + 1)
                for i in range(NT):
                    dve.wait_ge(ph_ok, NT * l + i + 1)
                    dve.tensor_tensor(pTlo[:, :, P * i:P * i + tok(i)],
                                      ps[:, i % 4, 0:2 * P].rearrange("p (k t) -> p k t", t=P)[:, :, 0:tok(i)],
                                      pThi[:, :, P * i:P * i + tok(i)].bitcast(f32), ALU.subtract).then_inc(pl_ok, 1)
                lo(U_P[l] + AHEAD)
                for i in range(2, NT + 1):
                    if i < NT:
                        stats_of(i)
                    if i > 2:
                        rstd_of(i - 1, n1 + i)
                    scale_of(i - 1, n1 + i)
                dve.wait_ge(wr_ld, 64 * (l + 1))
                dve.wait_ge(r_mm, NT * (l + 1))
                ch.link(dve.tensor_tensor(lg[:, :, :], ps[:, 0, 0:32 * NT].rearrange("p (t c) -> p t c", c=32)[:, :, 0:20],
                                          br[:, :].unsqueeze(1).to_broadcast([P, NT, 20]), ALU.add))
                minus4 = ovw[:, 5, 0:4].unsqueeze(1).to_broadcast([P, NT, 4])
                ch.link(dve.tensor_scalar(ovw[:, 5, 0:4], iota[:, 0:4], -4.0, None, ALU.add))
                dve.memset(m16[TS:P, 4, 0:1], 0.0).then_inc(m_ok, 1)
                gl = lg[:, :, 0:4]
                el = lg[:, :, 4:20].rearrange("p t (g j) -> p t g j", g=4)
                first_max(gl, ohg[:, :, :], 0)
                dve.tensor_tensor(r4[:, :, :], gl, s5[:, 0, :].unsqueeze(2).to_broadcast([P, NT, 4]), ALU.subtract).then_inc(r_ex, 1)
                ch.link(dve.tensor_tensor(t16[:, :, :, :], el, ohg[:, :, :].unsqueeze(3).to_broadcast([P, NT, 4, 4]), ALU.mult))
                ch.link(dve.tensor_reduce(out=ein[:, :, :], in_=t16.rearrange("p t g j -> p t j g"), op=ALU.add, axis=AX.X))
                first_max(ein[:, :, :], oh1[:, :, :], 1)
                ch.link(dve.scalar_tensor_tensor(out=ein[:, :, :], in0=oh1[:, :, :], scalar=-3.0e38, in1=ein[:, :, :], op0=ALU.mult, op1=ALU.add))
                first_max(ein[:, :, :], oh2[:, :, :], 2)
                dve.tensor_tensor(s5[:, 3, :], s5[:, 2, :], s5[:, 1, :], ALU.subtract).then_inc(r_ex, 1)
                for k, oh in enumerate((oh1, oh2)):
                    ins = dve.tensor_tensor(oh16[k], ohg[:, :, :].unsqueeze(3).to_broadcast([P, NT, 4, 4]),
                                            oh[:, :, :].unsqueeze(2).to_broadcast([P, NT, 4, 4]), ALU.mult)
                ch.link(ins)
                ch.link(dve.tensor_tensor(m16[:, :, :], oh16[0].rearrange("p t g j -> p t (g j)"), oh16[1].rearrange("p t g j -> p t (g j)"), ALU.add))
                dve.memset(m16[TS:P, 4, :], 0.0).then_inc(m_ok, 1)
                dve.wait_ge(r_ex_ok, 2 * (l + 1))
                ch.link(dve.tensor_reduce(out=s5[:, 4, :], in_=r4[:, :, :], op=ALU.add, axis=AX.X))
                ch.link(dve.scalar_tensor_tensor(out=s5[:, 5, :], in0=s5[:, 3, :], scalar=1.0, in1=s5[:, 4, :], op0=ALU.add, op1=ALU.mult))
                ch.link(dve.reciprocal(wtop[:, 0, :], s5[:, 5, :]))
                ch.link(dve.tensor_tensor(wtop[:, 1, :], wtop[:, 0, :], s5[:, 3, :], ALU.mult))
                dve.wait_ge(rank_ok, l + 1)
                rank = ps[:, 1, 0:NT * NE].rearrange("p (t e) -> p t e", e=NE)
                cnt = ps[:, 1, NT * NE:(NT + 1) * NE]
                ch.link(dve.memset(ovw[:, 0:4, 0:8], 0.0))
                ch.link(dve.tensor_scalar(ovw[:, 0, 8:24], cnt, 128.0, None, ALU.is_gt))
                for n in (256.0, 384.0, 512.0):
                    ch.link(dve.scalar_tensor_tensor(out=ovw[:, 0, 8:24], in0=cnt, scalar=n, in1=ovw[:, 0, 8:24], op0=ALU.is_gt, op1=ALU.add))
                a = 0
                for step, b in ((1, 1), (2, 2), (4, 1), (8, 2)):
                    ch.link(dve.tensor_tensor(ovw[:, b, 8:24], ovw[:, a, 8:24], ovw[:, a, 8 - step:24 - step], ALU.add))
                    a = b
                incl = ovw[:, 2, 8:24]
                ch.link(dve.tensor_tensor(ovw[:, 3, 8:24], incl, ovw[:, 0, 8:24], ALU.subtract))
                ch.link(dve.tensor_scalar(ovw[:, 3, 8:24], ovw[:, 3, 8:24], 128.0, float(NE * CAP - CAP), ALU.mult, ALU.add))
                ch.link(dve.tensor_tensor(ovw[:, 3, 8:24], ovw[:, 3, 8:24], iota_e[:, :], ALU.subtract))
                ch.link(dve.tensor_scalar(post[:, :, :], rank, 128.0, None, ALU.is_ge))
                ch.link(dve.tensor_tensor(post[:, :, :], post[:, :, :], ovw[:, 3, 8:24].unsqueeze(1).to_broadcast([P, NT, NE]), ALU.mult))
                ch.link(dve.tensor_tensor(post[:, :, :], post[:, :, :], rank, ALU.add))
                ch.link(dve.tensor_tensor(post[:, :, :], post[:, :, :], iota_e[:, :].unsqueeze(1).to_broadcast([P, NT, NE]), ALU.add))
                for k in range(2):
                    ch.link(dve.tensor_tensor(t16.rearrange("p t g j -> p t (g j)"), oh16[k].rearrange("p t g j -> p t (g j)"), post[:, :, :], ALU.mult))
                    ch.link(dve.tensor_reduce(out=pmd[:, 0, NT * k:NT * k + NT], in_=t16.rearrange("p t g j -> p t (g j)"), op=ALU.add, axis=AX.X))
                dve.tensor_copy(pos_u[:, :, :].rearrange("p t k -> p k t"), pmd[:, 0, :].rearrange("p (k t) -> p k t", k=2)).then_inc(idx_ok, 1)
                ch.link(dve.tensor_copy(posi[:, 0, :], pmd[:, 0, :]))
                ch.link(dve.tensor_single_scalar(posi[:, 1, :], posi[:, 0, :], CAP - 1, op=ALU.bitwise_and))
                ch.link(dve.tensor_single_scalar(posi[:, 2, :], posi[:, 0, :], 7, op=ALU.arith_shift_right))
                ch.link(dve.tensor_copy(pmd[:, 1:3, :], posi[:, 1:3, :]))
                for n in range(2 * NT):
                    if n >= 2:
                        dve.wait_ge(ab_used, 2 * NT * l + n - 1)
                    dve.tensor_scalar(amat[:, n % 2, :], iota[:, :], pmd[:, 1, n:n + 1], None, ALU.is_equal)
                    dve.tensor_scalar(bmat[:, n % 2, :], iota[:, 0:SLOT_TILES], pmd[:, 2, n:n + 1],
                                      tokid[:, n % NT:n % NT + 1], ALU.is_equal, ALU.mult).then_inc(ab_ok, 1)
                ch.link(dve.tensor_tensor(wide[0:1, :, :], incl[0:1].unsqueeze(1).to_broadcast([1, OVF, NE]),
                                          iota[0:1, 0:OVF].unsqueeze(2).to_broadcast([1, OVF, NE]), ALU.is_le))
                ch.link(dve.tensor_reduce(out=ovw[0:1, 4, 0:OVF], in_=wide[0:1, :, :], op=ALU.add, axis=AX.X))
                dve.tensor_scalar(ovf_e[:, :], ovw[0:1, 4, 0:OVF], float(NE - 1), None, ALU.min)
                dve.tensor_copy(n_ovf[:, :], incl[0:1, NE - 1:NE]).then_inc(idx_ok, 1)
                dve.wait_ge(ab_used, 2 * NT * (l + 1))
                dve.tensor_copy(idx[:, :], ps[:, 6, 0:SLOT_TILES]).then_inc(idx_ok, 1)

                def xT_lo(s, it=0, step=0):
                    q = it * (2 * step) + 2 * (NE * l + s)
                    for b in range(2):
                        dve.wait_ge(eth_ok, q + (b + 1))
                        dve.tensor_tensor(eTl[:, 512 * b:512 * b + 512], ps[:, 2 + b, :], eTh[:, 512 * b:512 * b + 512].bitcast(f32),
                                          ALU.subtract).then_inc(etl_ok, 1)

                def expert_lo(e, it, step):
                    if e < EU:
                        lo(U_E[l] + e, it, 3 * step)

                def moe_step(s, it=0, step=0):
                    e = 3 * s + 2
                    expert_lo(e, it, step)
                    expert_lo(e + 1, it, step)
                    if s < NE:
                        q = it * step + (NE * l + s)
                        dve.wait_ge(si_ok, q + 1)
                        if l or s or step:
                            dve.wait_ge(at_ok, q)
                        dve.tensor_tensor(act_a[:, 1, :], act_a[:, 0, :], ps[:, 0, F:2 * F], ALU.mult).then_inc(a_ok, 1)
                    if s < NE - 1:
                        xT_lo(s + 1, it, step)
                        expert_lo(e + 2, it, step)
                    if s < NE:
                        dve.wait_ge(ath_ok, q + 1)
                        dve.tensor_tensor(aTl[:, :], ps[:, 1, 0:F], aTh[:, :].bitcast(f32), ALU.subtract).then_inc(atl_ok, 1)

                lo(U_E[l])
                lo(U_E[l] + 1)
                xT_lo(0)
                moe_step(0)
                moe_step(1)
                with dve.Fori(0, 3) as it:
                    for s in range(2, 6):
                        moe_step(s, it, 4)
                for s in range(NE - 2, NE + 1):
                    moe_step(s)
                n = dve.value_load(n_ovf[0:1, 0:1], min_val=0, max_val=OVF)
                with dve.If(n > 0):
                    o = ov[l]
                    with dve.Fori(0, OVF) as i:
                        dve.wait_ge(o["silu"], i + 1)
                        dve.tensor_tensor(act_a[:, 1, :], act_a[:, 0, :], ps[:, 0, F:2 * F], ALU.mult).then_inc(o["a"], 1)
                for j in range(AHEAD):
                    lo(U_G[l] + j)
                n2 = n1 + NT
                dve.wait_ge(ln_ld, 32 * (2 * l + 2))
                dve.wait_ge(xs_ok, l + 1)
                for i in range(NT + 2):
                    if i < NT:
                        t = tok(i)
                        dve.wait_ge(yg_ld[i % 2], 32 * ((3 if i % 2 == 0 else 2) * l + i // 2 + 1))
                        for k in range(2):
                            ch.link(dve.scalar_tensor_tensor(out=xtok[0:t, i, :], in0=yg[0:t, i % 2, k, :], scalar=wtop[0:t, k, i:i + 1],
                                                             in1=xtok[0:t, i, :], op0=ALU.mult, op1=ALU.add))
                        for h in range(2):
                            ins = dve.bn_stats(vstat[:, i, h, :], xtok[:, i, 512 * h:512 * h + 512])
                        ch.link(ins)
                        dve.bn_aggr(mv[:, i, :], vstat[:, i, 0:2, :].rearrange("p a b -> p (a b)")).then_inc(st_ok, 1)
                    if 1 <= i <= NT:
                        rstd_of(i - 1, n2 + i)
                    if i >= 2:
                        scale_of(i - 2, n2 + i - 1)

                def x_lo(n):
                    for k in range(KT):
                        dve.wait_ge(xhi_ok, n + k + 1)
                        dve.tensor_tensor(xk(xlo, k, 0, T), xk(xT, k, 0, T), xk(xhi, k, 0, T).bitcast(f32), ALU.subtract).then_inc(xlo_ok, 1)

                x_lo(NT + 1 + 2 * KT * l)
                for j in range(4):
                    if U_G[l] + j + AHEAD < U_END:
                        lo(U_G[l] + j + AHEAD)
                    for m in range(2):
                        mo = 2 * j + m
                        dve.wait_ge(sg_ok, KT * l + mo + 1)
                        ch.link(dve.tensor_tensor(sgm[:, m, :], sgm[:, m, :], ppT[:, mo, :], ALU.mult))
                        dve.tensor_tensor(xk(xT, mo, 0, T), xk(xT, mo, 0, T), sgm[:, m, :], ALU.add).then_inc(pe_ok, 1)
                if l == 0:
                    x_lo(NT + 1 + KT)
                    dve.wait_ge(xlo_ok, NT + 1 + 2 * KT)
                    ch.link(dve.tensor_scalar(xT[:, :], xT[:, :], ALPHA, None, ALU.mult))
                    dve.wait_ge(past_t, 1)
                    ch.link(dve.tensor_copy(pastT[:, :, :], ps[:, 6, 0:KT * RB * 2].rearrange("p (k c) -> p k c", k=KT)))
                    for m in range(2):
                        ins = dve.memset(cx[:, m, 0:2], 0.0)
                    ch.link(ins)

                    def conv_tile(f, m):
                        own = cx[:, m, 2 + TP:].rearrange("p (b t) -> p b t", t=2 + SB)
                        dve.tensor_copy(own[:, :, 0:2], pastT[:, f, :].rearrange("p (b w) -> p b w", w=2))
                        for h, (c0, c1) in enumerate(((0, HALF), (HALF, TP))):
                            dve.tensor_tensor(cx[:, m, 2 + c0:2 + c1], c_sb[:, m, c0:c1], ps[:, 2 * m + h, c0 - HALF * h:c1 - HALF * h], ALU.mult)
                        dve.tensor_tensor(own[:, :, 2:], c_sb[:, m, TP:T].rearrange("p (b t) -> p b t", t=SB),
                                          ps[:, 2 * m + 1, TP - HALF:HALF].rearrange("p (b t) -> p b t", t=SB), ALU.mult).then_inc(cx_ok, 1)
                        dve.wait_ge(cx_ok, f + 1)
                        o_p, o_s = conv[:, f, 0:TP], conv[:, f, TP:T].rearrange("p (b t) -> p b t", t=SB)
                        w = [cols[:, C_CW + KT * n + f:C_CW + KT * n + f + 1] for n in range(3)]
                        dve.tensor_scalar(o_p, cx[:, m, 0:TP], w[0], None, ALU.mult)
                        ch.link(dve.tensor_scalar(o_s, own[:, :, 0:SB], w[0], None, ALU.mult))
                        for n in (1, 2):
                            dve.scalar_tensor_tensor(out=o_p, in0=cx[:, m, n:n + TP], scalar=w[n], in1=o_p, op0=ALU.mult, op1=ALU.add)
                            ch.link(dve.scalar_tensor_tensor(out=o_s, in0=own[:, :, n:n + SB], scalar=w[n], in1=o_s, op0=ALU.mult, op1=ALU.add))
                        dve.tensor_copy(last[:, f, 0:2], cx[:, m, TP:TP + 2])
                        dve.tensor_copy(last[:, f, 2:].rearrange("p (b w) -> p b w", w=2), own[:, :, SB:SB + 2]).then_inc(last_ok, 1)

                    for jj in range(4):
                        lo(U_CH + 2 * jj + AHEAD)
                        for m in range(2):
                            dve.wait_ge(c_ok, 2 * jj + m + 1)
                            dve.wait_ge(mt_done, M_CH + 4 * jj + 2 + m + 1)
                            conv_tile(2 * jj + m, m)
                        lo(U_CH + 2 * jj + 1 + AHEAD)
                    for r in range(BR):
                        for fl in range(ROUND):
                            q = ROUND * (AR + r) + fl
                            dve.wait_ge(mt_done, M_B + 12 * r + fl + 1)
                            dve.tensor_tensor(halves(gf[:, fl % 2, :]), halves(conv[:, ROUND * r + fl, :]), pair(fl % 2), ALU.mult).then_inc(gm_done, 1)
                            g_low(q, fl)
                            if fl < 3:
                                lo(U_B + 4 * r + fl + AHEAD)
                        for mo in range(KT):
                            if mo == 6:
                                lo(U_B + 4 * r + 3 + AHEAD)
                            add_out(M_B + 12 * r, KT * (AR + r), mo)

        @block.tensor
        def _(pe):
            pe_pairs = [0]

            def turn_rows(n, src, wait=None, value=0):
                b = turned_bank(n)
                for k in range(KT):
                    ins = pe.transpose(ps[:, b + k // 4, (k % 4) * P:(k % 4) * P + P], src[:, k * P:k * P + P], ident[:, :])
                ins.then_inc(tr_done, 1)

            def turn_cols(n, i):
                b = turned_bank(n)
                for k in range(KT):
                    ins = pe.transpose(ps[:, b + k // 4, (k % 4) * P:(k % 4) * P + P], xk(xT, k, P * i, P), ident[:, :])
                ins.then_inc(tr_done, 1)

            def products(out, terms):
                for n, (sh, sl, mh, ml) in enumerate(terms):
                    first, final = n == 0, n == len(terms) - 1
                    pe.matmul(out, sh, mh, start=first, stop=False)
                    pe.matmul(out, sh, ml, start=False, stop=False)
                    ins = pe.matmul(out, sl, mh, start=False, stop=final)
                return ins

            def dense_tile(par, j, c0, kn, wview, xh_, xl_, xview, used=False):
                for h in range(2):
                    ins = products(ps[:, 2 * par + h, 0:HALF],
                                   [(wview(whi, j, k, c0), wview(wlo, j, k, c0), xview(xh_, k, h), xview(xl_, k, h)) for k in range(kn)])
                return ins

            def xview(x, k, h):
                return xk(x, k, HALF * h, HALF)

            def gview(g, k, h):
                return g[:, k, HALF * h:HALF * h + HALF]

            pe.wait_ge(const_ok, 1)
            pe.wait_ge(x_ld, 32)
            for i in range(NT):
                if i >= 2:
                    pe.wait_ge(tr_free, i - 1)
                turn_rows(TR_IN + i, xtok[:, i, :])
            pe.wait_ge(small_ld, 48)
            pe.wait_ge(ws_ld, 32)
            pe.transpose(ps[:, 0, 0:64], colsrc[:, :], ident[0:64, 0:64])
            for h in range(NH):
                ins = pe.transpose(ps[:, 1, h * P:h * P + P], wsrc[:, h, :], ident[:, :])
            ins.then_inc(ws_t, 1)
            pe.wait_ge(ws_cp, 1)

            pe.wait_ge(xlo_ok, NT + 1)

            def v_unit(n, j, it=0, step=0):
                pe.wait_ge(split_done, it * step + (n + 1))
                for i in range(NT):
                    q = NT * n + i
                    if q >= 4 or step:
                        pe.wait_ge(vz_done, it * (NT * step) + (q - 3))
                    products(ps[:, q % 4, 0:256],
                             [(xk(xhi, k, P * i, P), xk(xlo, k, P * i, P), w8(whi, j, k, 0, 256), w8(wlo, j, k, 0, 256))
                              for k in range(KT)]).then_inc(vps_done, 1)

            for n in range(4):
                v_unit(n, n)
            with pe.Fori(0, VU // 4 - 1) as it:
                for j in range(4):
                    v_unit(4 + j, j, it, 4)
            pe.wait_ge(vz_done, V_DONE)

            pe.wait_ge(bsl_ld, 16)
            pe.wait_ge(ones_ok, 1)
            pe.wait_ge(blk_ld, 16 * RB)

            def spatial(r, fl, it, step):
                q = it * (ROUND * step) + (ROUND * r + fl)
                if fl == 0:
                    pe.wait_ge(vn_ok, it * (NT * step) + NT * (r + 1))
                if r or step or fl >= 2:
                    pe.wait_ge(gm_done, q - 1)
                b = 4 + 2 * (fl % 2)
                half = it * (2 * step) + (2 * r + fl // 2)
                h = (half * 11) // 32
                for c in range(4):
                    out = ps[:, b, P * c:P * c + P]
                    pe.matmul(out, ones_r[:, :], bsx[:, ds(h, 1), 0:P].rearrange("p a t -> p (a t)"), start=True, stop=False)
                    pe.matmul(out, vc[:, c, P * fl:P * fl + P], wst[:, ds(h, 1), :].rearrange("p a t -> p (a t)"), start=False, stop=True)
                out = ps[:, b + 1, 0:TS]
                pe.matmul(out, ones_r[:, :], bsx[:, ds(h, 1), P:].rearrange("p a t -> p (a t)"), start=True, stop=False)
                pe.matmul(out, vc[0:TS, 4, P * fl:P * fl + P], wss[:, ds(h, 1), :].rearrange("p a t -> p (a t)"),
                          start=False, stop=True).then_inc(sg_done, 1)

            def a_round(r, it, step):
                for fl in range(ROUND):
                    spatial(r, fl, it, step)
                    if fl % 2 == 0:
                        pe.wait_ge(split_done, it * (4 * step) + (U_A + 4 * r + fl // 2 + 1))
                    if fl >= 2:
                        pe.wait_ge(u_done, it * (ROUND * step) + (ROUND * r + fl - 1))
                    elif r or step:
                        pe.wait_ge(o_done, it * (KT * step) + (KT * r - 1 + fl))
                    dense_tile(fl % 2, fl // 2, P * (fl % 2), KT, w8, xhi, xlo, xview).then_inc(mt_done, 1)
                out_tiles(it * (ROUND * step) + ROUND * (r + 1), u_done, it * (ROUND * step) + ROUND * (r + 1),
                          it * (KT * step) + KT * r, it * (4 * step) + (U_A + 4 * r + 2))

            def out_tiles(gl_n, pair_sem, pair_n, o0, d):
                pe.wait_ge(gl_done, gl_n)
                for mo in range(KT):
                    if mo % 4 == 0:
                        pe.wait_ge(split_done, d + (mo // 4 + 1))
                    if mo < 2:
                        pe.wait_ge(pair_sem, pair_n + (mo - 1))
                    else:
                        pe.wait_ge(o_done, o0 + (mo - 1))
                    dense_tile(mo % 2, 2 + mo // 4, P * (mo % 4), ROUND, w4, ghi, glo, gview).then_inc(mt_done, 1)

            a_round(0, 0, 0)
            with pe.Fori(0, AR - 1) as it:
                a_round(1, it, 1)

            for l in range(DEPTH):
                o_all = KT * (AR + BR * l)
                pe.wait_ge(o_done, o_all)

                def n1_turn(i):
                    if i >= 2:
                        pe.wait_ge(nz_ok, 2 * NT * l + i - 1)
                    turn_cols(TR_N1[l] + i, i)

                n1_turn(0)
                n1_turn(1)
                pe.wait_ge(p_ld, 32 * (l + 1))
                for i in range(NT):
                    if i == 4:
                        pe.wait_ge(pl_ok, NT * l + 1)
                    for k in range(2):
                        ins = pe.transpose(ps[:, i % 4, k * P:k * P + tok(i)], p_tok[0:tok(i), i, k * P:k * P + P], ident[0:tok(i), 0:tok(i)])
                    ins.then_inc(p_turn, 1)
                for i in range(2, NT):
                    n1_turn(i)

                def pview(p, k, h):
                    return p[:, k, HALF * h:HALF * h + HALF]

                def proj(mo):
                    if mo % 2 == 0:
                        pe.wait_ge(split_done, U_P[l] + mo // 2 + 1)
                    if mo >= 2:
                        pe.wait_ge(pp_done, KT * l + mo - 1)
                    dense_tile(mo % 2, mo // 2, P * (mo % 2), 2, w8, pThi, pTlo, pview).then_inc(mt_done, 1)

                pe.wait_ge(pl_ok, NT * (l + 1))
                for mo in range(4):
                    proj(mo)
                pe.wait_ge(wr_ld, 64 * (l + 1))
                for i in range(NT):
                    if i < 2:
                        pe.wait_ge(nz_ok, 2 * NT * l + NT)
                    else:
                        pe.wait_ge(tr_free, TF_RT[l] + i - 1)
                    pe.wait_ge(nb_ok, 2 * NT * l + i + 1)
                    turn_rows(TR_RT[l] + i, xtok[:, i, :])
                    if i == 0:
                        pe.wait_ge(pp_done, KT * l + 4)
                    pe.wait_ge(tr_free, TF_RT[l] + i + 1)
                    for k in range(KT):
                        ins = pe.matmul(ps[:, 0, 32 * i:32 * i + 20], x1T[:, k, :], wr[:, k, :], start=(k == 0), stop=(k == KT - 1))
                    ins.then_inc(r_mm, 1)
                pe.wait_ge(m_ok, 2 * l + 1)
                for mo in range(4, 8):
                    proj(mo)
                pe.wait_ge(pp_done, KT * (l + 1))
                pe.wait_ge(m_ok, 2 * l + 2)
                for i in range(NT):
                    for j in range(i + 1):
                        pe.matmul(ps[:, 1, NE * i:NE * i + NE], below[:, :] if j == i else ones[:, :], m16[:, j, :],
                                  start=(j == 0), stop=(j == i))
                for j in range(NT):
                    ins = pe.matmul(ps[:, 1, NE * NT:NE * NT + NE], ones[:, :], m16[:, j, :], start=(j == 0), stop=(j == NT - 1))
                ins.then_inc(rank_ok, 1)
                for n in range(2 * NT):
                    pe.wait_ge(ab_ok, 2 * NT * l + n + 1)
                    ins = pe.matmul(ps[:, 6, 0:SLOT_TILES], amat[:, n % 2, :], bmat[:, n % 2, :], start=(n == 0), stop=(n == 2 * NT - 1))
                    ins.then_inc(ab_used, 1)

                def turn_slots(s, it=0, step=0, par=0):
                    pe.wait_ge(xg_ld[par], it * (8 * step) + 16 * ((NE // 2) * l + s // 2 + 1))
                    if l or s or step:
                        pe.wait_ge(etl_ok, it * (2 * step) + 2 * (NE * l + s))
                    for k in range(KT):
                        ins = pe.transpose(ps[:, 2 + k // 4, (k % 4) * P:(k % 4) * P + P], xg[:, par, k * P:k * P + P], ident[:, :])
                        if k % 4 == 3:
                            ins.then_inc(xtp, 1)

                def gate_up(s, it=0, step=0):
                    q = it * step + (NE * l + s)
                    pe.wait_ge(etl_ok, q * 2 + 2)
                    if l or s or step:
                        pe.wait_ge(a_ok, q)
                    for a in range(2):
                        e = gu_unit(s) + a
                        pe.wait_ge(split_done, it * (3 * step) + (U_E[l] + e + 1))
                        for k in range(4):
                            xs = [x[:, (4 * a + k) * P:(4 * a + k) * P + P] for x in (eTh, eTl)]
                            ws = [w[:, e % 4, 512 * k:512 * k + 512] for w in (whi, wlo)]
                            pe.matmul(ps[:, 0, :], xs[0], ws[0], start=(a == 0 and k == 0), stop=False)
                            pe.matmul(ps[:, 0, :], xs[0], ws[1], start=False, stop=False)
                            ins = pe.matmul(ps[:, 0, :], xs[1], ws[0], start=False, stop=(a == 1 and k == 3))
                        ins.then_inc(eu_used, 1)

                def down(s, it=0, step=0):
                    q = it * step + (NE * l + s)
                    pe.wait_ge(atl_ok, q + 1)
                    if l or s or step:
                        pe.wait_ge(y_cp, q)
                    e = dn_unit(s)
                    pe.wait_ge(split_done, it * (3 * step) + (U_E[l] + e + 1))
                    for a in range(2):
                        for h in range(2):
                            out = ps[:, 4 + h, :]
                            th, tl = aTh[:, P * a:P * a + P], aTl[:, P * a:P * a + P]
                            wh, wl = [w[:, e % 4, D * a + 512 * h:D * a + 512 * h + 512] for w in (whi, wlo)]
                            pe.matmul(out, th, wh, start=(a == 0), stop=False)
                            pe.matmul(out, th, wl, start=False, stop=False)
                            ins = pe.matmul(out, tl, wh, start=False, stop=(a == 1))
                    ins.then_inc(eu_used, 1)

                def turn_act(s, it=0, step=0):
                    q = it * step + (NE * l + s)
                    pe.wait_ge(a_ok, q + 1)
                    if l or s or step:
                        pe.wait_ge(atl_ok, q)
                    for c in range(2):
                        ins = pe.transpose(ps[:, 1, P * c:P * c + P], act_a[:, 1, P * c:P * c + P], ident[:, :])
                    ins.then_inc(at_ok, 1)

                def moe_step(s, it=0, step=0):
                    if s < NE:
                        gate_up(s, it, step)
                    if s < NE - 1:
                        turn_slots(s + 1, it, step, (s + 1) % 2)
                    if s >= 1 or step:
                        down(s - 1, it, step)
                    if s < NE:
                        turn_act(s, it, step)

                pe.wait_ge(idx_ok, 3 * (l + 1))
                turn_slots(0)
                moe_step(0)
                moe_step(1)
                with pe.Fori(0, 3) as it:
                    for s in range(2, 6):
                        moe_step(s, it, 4)
                for s in range(NE - 2, NE + 1):
                    moe_step(s)
                n = pe.value_load(n_ovf[0:1, 0:1], min_val=0, max_val=OVF)
                with pe.If(n > 0):
                    o = ov[l]
                    wgu = raw[:, 0:2, :].rearrange("p a (k c) -> p (a k) c", c=2 * F)
                    wdn = raw[:, 2, :].rearrange("p (k c) -> p k c", c=D)
                    pe.wait_ge(y_cp, NE * (l + 1))
                    with pe.Fori(0, OVF) as i:
                        pe.wait_ge(ovx_ld[l], i * 16 + 16)
                        for k in range(KT):
                            ins = pe.transpose(ps[:, 2 + k // 4, (k % 4) * P:(k % 4) * P + P], xg[:, 0, k * P:k * P + P], ident[:, :])
                        ins.then_inc(o["turned"], 1)
                        pe.wait_ge(o["copied"], i + 1)
                        pe.wait_ge(ov_ld[l], i * 48 + 48)
                        for k in range(KT):
                            ins = pe.matmul(ps[:, 0, :], eTf[:, k * P:k * P + P], wgu[:, k, :], start=(k == 0), stop=(k == KT - 1))
                        ins.then_inc(o["gu"], 1)
                        pe.wait_ge(o["a"], i + 1)
                        for c in range(2):
                            ins = pe.transpose(ps[:, 1, P * c:P * c + P], act_a[:, 1, P * c:P * c + P], ident[:, :])
                        ins.then_inc(o["aturned"], 1)
                        pe.wait_ge(o["acopied"], i + 1)
                        for h in range(2):
                            for k in range(2):
                                ins = pe.matmul(ps[:, 4 + h, :], aTf[:, k * P:k * P + P], wdn[:, k, 512 * h:512 * h + 512],
                                                start=(k == 0), stop=(k == 1))
                        ins.then_inc(o["y"], 1)
                        pe.wait_ge(o["ycopied"], i + 1)
                pe.wait_ge(y_cp, NE * (l + 1))
                for i in range(NT):
                    if i >= 2:
                        pe.wait_ge(tr_free, TF_N2[l] + i - 1)
                    pe.wait_ge(nb_ok, 2 * NT * l + NT + i + 1)
                    turn_rows(TR_N2[l] + i, xtok[:, i, :])
                pe.wait_ge(atl_ok, NE * (l + 1))
                pe.wait_ge(xlo_ok, NT + 1 + 2 * KT * l + KT)
                for mo in range(KT):
                    if mo % 2 == 0:
                        pe.wait_ge(split_done, U_G[l] + mo // 2 + 1)
                    if mo >= 2:
                        pe.wait_ge(sg_ok, KT * l + mo - 1)
                    dense_tile(mo % 2, mo // 2, P * (mo % 2), KT, w8, xhi, xlo, xview).then_inc(mt_done, 1)
                if l == 0:
                    pe.wait_ge(past_ld, 16)
                    for k in range(KT):
                        ins = pe.transpose(ps[:, 6, 2 * RB * k:2 * RB * k + 2 * RB], past[:, k * P:k * P + P], ident[0:2 * RB, 0:2 * RB])
                    ins.then_inc(past_t, 1)
                    pe.wait_ge(xlo_ok, NT + 1 + 2 * KT)
                    for jj in range(4):
                        for part in range(2):
                            pe.wait_ge(split_done, U_CH + 2 * jj + part + 1)
                            for m in range(2):
                                if part:
                                    pe.wait_ge(c_ok, 2 * jj + m + 1)
                                elif jj:
                                    pe.wait_ge(cx_ok, 2 * jj - 1 + m)
                                else:
                                    pe.wait_ge(sg_ok, KT)
                                dense_tile(m, (2 * jj + part) % 4, P * m, KT, w8, xhi, xlo, xview).then_inc(mt_done, 1)
                    for r in range(BR):
                        for fl in range(ROUND):
                            if fl % 2 == 0:
                                pe.wait_ge(split_done, U_B + 4 * r + fl // 2 + 1)
                            if fl >= 2:
                                pe.wait_ge(gm_done, ROUND * (AR + r) + fl - 1)
                            elif r:
                                pe.wait_ge(o_done, KT * (AR + r) - 1 + fl)
                            else:
                                pe.wait_ge(cx_ok, KT - 1 + fl)
                            dense_tile(fl % 2, fl // 2, P * (fl % 2), KT, w8, xhi, xlo, xview).then_inc(mt_done, 1)
                        out_tiles(ROUND * (AR + r + 1), gm_done, ROUND * (AR + r + 1), KT * (AR + r), U_B + 4 * r + 2)
                        if r == 0:
                            pe.wait_ge(last_ok, KT)
                            for k in range(KT):
                                ins = pe.transpose(ps[0:18, 6 + k // 4, (k % 4) * P:(k % 4) * P + P], last[:, k, :], ident[:, :])
                            ins.then_inc(last_t, 1)
                    pe.wait_ge(last_cp, 1)
            pe.wait_ge(pe_ok, 2 * KT)
            for i in range(NT):
                if i >= 2:
                    pe.wait_ge(out_cp, i - 1)
                turn_cols(TR_OUT + i, i)


_OUTS = [((1, TP, D), "float32"), ((RB, SB, D), "float32"), ((1, 1, P, AW), "float32"),
         ((1, RB, SB, AW), "float32"), ((1, 1, 2, D), "float32"), ((1, RB, 2, D), "float32")]


def kernel(**inputs):
    import numpy as _np
    import concourse.bacc as _bacc
    from concourse import mybir as _mybir
    from concourse.bass_utils import run_bass_kernel_spmd as _run

    nc = _bacc.Bacc("TRN2", target_bir_lowering=False, num_devices=1)
    arrays, ins, outs = {}, {}, []
    for name, a in inputs.items():
        a = _np.ascontiguousarray(a)
        arrays[f"in_{name}"] = a
        ins[name] = nc.dram_tensor(f"in_{name}", a.shape, _mybir.dt.from_np(a.dtype), kind="ExternalInput").ap()
    for i, (shape, dtype) in enumerate(_OUTS):
        outs.append(nc.dram_tensor(f"out_{i}", shape, _mybir.dt.from_np(_np.dtype(dtype)), kind="ExternalOutput").ap())
    trunk(nc, ins, outs)
    r = _run(nc, [arrays], core_ids=[0])
    return tuple(r.results[0][f"out_{i}"] for i in range(len(_OUTS)))
```

```python
import concourse.bass as bass
from concourse import mybir
from contextlib import ExitStack

P = 128
D = 1024
KT = D // P
TP, TS = 512, 64
T = TP + TS
NT = 5
HALF = T // 2
AW = 3072
NH = 4
NE = 16
F = 256
PLE = 256
RB, SB = 8, 8
DEPTH = 2
EPS = 1e-5
ALPHA = float((2 * DEPTH) ** 0.25)
UNIT = 2048
CAP = 128
OVF = 8
SLOT_TILES = NE + OVF
ROUND = 4
AR = AW // P // ROUND
BR = KT // ROUND
VU = AW // 256
U_V = 0
U_A = U_V + VU
U_P = [U_A + 4 * AR, 0]
U_E = [U_P[0] + 4, 0]
EU = 3 * NE
U_G = [U_E[0] + EU, 0]
U_CH = U_G[0] + 4
U_B = U_CH + 8
U_P[1] = U_B + 4 * BR
U_E[1] = U_P[1] + 4
U_G[1] = U_E[1] + EU
U_END = U_G[1] + 4
M_A = 0
M_P = [12 * AR, 0]
M_G = [M_P[0] + 8, 0]
M_CH = M_G[0] + 8
M_B = M_CH + 16
M_P[1] = M_B + 12 * BR
M_G[1] = M_P[1] + 8
AHEAD = 3


class Chain:

    def __init__(self, eng, sem):
        self.eng, self.sem, self.base, self.k, self.it, self.per = eng, sem, 0, 0, 0, 0

    def enter(self, it, per):
        self.base, self.it, self.per, self.k = self.base + self.k, it, per, 0

    def leave(self, n):
        assert self.k == self.per, (self.k, self.per)
        self.base, self.k, self.it, self.per = self.base + self.per * n, 0, 0, 0

    def link(self, ins):
        self.k += 1
        ins.then_inc(self.sem, 1)
        self.eng.wait_ge(self.sem, self.base + self.k + (self.it * self.per if self.per else 0))


def trunk(nc, x_in, outs):
    f32, f32r, i32, u32 = mybir.dt.float32, mybir.dt.float32r, mybir.dt.int32, mybir.dt.uint32
    ACT, ALU, AX = mybir.ActivationFunctionType, mybir.AluOpType, mybir.AxisListType
    ds = bass.ds

    x_prompt = x_in["x_prompt"][0].rearrange("(i p) d -> p i d", p=P)
    x_sample = x_in["x_sample"].rearrange("b s d -> (b s) d")
    w_in = x_in["a_w_in"][0]
    w_out = x_in["a_w_out"][0]
    bw_in = x_in["b_w_in"][0]
    bw_out = x_in["b_w_out"][0]
    v_dram = nc.dram_tensor("v_scratch", (NT, P, AW), f32).ap()
    x_dram = [nc.dram_tensor(f"x_scratch{l}", (T, D), f32).ap() for l in range(DEPTH)]
    y_dram = [nc.dram_tensor(f"y_scratch{l}", (SLOT_TILES * CAP, D), f32).ap() for l in range(DEPTH)]
    y_prompt = outs[0][0].rearrange("(i p) d -> p i d", p=P)
    y_sample = outs[1].rearrange("b s d -> (b s) d")
    v_state_p = outs[2][0, 0]
    v_state_s = outs[3][0].rearrange("b s d -> (b s) d")
    conv_state_p = outs[4][0, 0]
    conv_state_s = outs[5][0].rearrange("b s d -> (b s) d")

    top = [(nc.sbuf_base + 63) // 64 * 64]

    def at(name, shape, dt, off):
        return nc.alloc_sbuf_tensor_at(name, shape, dt, offset=off)

    def new(name, shape, dt=f32):
        n = 4
        for s in shape[1:]:
            n *= s
        off = top[0]
        top[0] += (n + 31) // 32 * 32
        return at(name, shape, dt, off)

    NCOL = 96
    XCOLS = KT * T + 64
    raw = new("w_raw", [P, 4, UNIT])
    whi = new("w_hi", [P, 4, UNIT], f32r)
    wlo = new("w_lo", [P, 4, UNIT], f32r)
    xT = new("xT", [P, XCOLS])
    XH0 = top[0]
    xhi = new("x_hi", [P, XCOLS], f32r)
    xlo = new("x_lo", [P, XCOLS], f32r)
    XH1 = top[0]
    ident = new("ident", [P, P])
    below = new("below", [P, P])
    ones = new("ones", [P, P])
    ones_r = new("ones_r", [P, P], f32r)
    iota = new("iota", [P, P])
    tokid = new("tokid", [P, NT])
    iota_e = new("iota_e", [P, NE])
    eps = new("eps", [P, 1])
    cols = new("cols", [P, NCOL])
    wst = new("w_spatial", [P, NH, P])
    wss = new("w_spatial_s", [TS, NH, TS])
    bsx = new("b_spatial", [P, NH, P + TS], f32r)
    vstat = new("v_stats", [P, NT, VU, 6])
    mv = new("mean_var", [P, NT, 2])
    rstd = new("rstd", [P, NT])
    nmr = new("neg_mean_rstd", [P, NT])
    idx = new("slot_token", [P, SLOT_TILES], u32)
    pos_u = new("token_slot", [P, NT, 2], u32)
    wtop = new("top_weights", [P, 2, NT])
    n_ovf = new("n_overflow", [1, 1], i32)
    ovf_e = new("overflow_expert", [1, OVF], i32)
    S0 = top[0]

    C_BU, C_BG, C_CW, C_G2, C_B2 = 0, 24, 40, 64, 80
    xtok = at("x_tok", [P, NT, D], f32, S0)
    colsrc = at("cols_src", [NCOL, P], f32, S0 + 20480)
    wsrc = at("w_spatial_src", [P, NH, P], f32, S0 + 20992)
    bsrc = at("b_spatial_src", [1, NH, P], f32, S0 + 23040)
    bss = at("b_spatial_all", [1, NH, P + TS], f32, S0 + 25088)
    bsl = at("b_spatial_low", [1, NH, P + TS], f32r, S0 + 28160)
    vst = at("v_stage", [P, 2, NT, 256], f32, S0)
    bvb = at("v_bias", [P, AW], f32, S0 + 35104)
    ghi = at("g_hi", [P, ROUND, T], f32r, S0)
    glo = at("g_lo", [P, ROUND, T], f32r, S0 + 9216)
    gf = at("g_full", [P, 2, T], f32, S0 + 18432)
    vc = at("v_cols", [P, NT, 512], f32, S0 + 23040)
    gb = at("v_ln", [P, 2, 512], f32, S0 + 33280)
    conv = at("conv", [P, KT, T], f32, S0 + 23200)
    HP = 2 + TP + RB * (2 + SB)
    cx = at("conv_in", [P, 2, HP], f32, S0 + 18432)
    c_sb = at("c_gate", [P, 2, T], f32, S0)
    past = at("past_src", [RB * 2, D], f32, S0 + 4608)
    pastT = at("pastT", [P, KT, RB * 2], f32, S0 + 8704)
    last = at("conv_last", [P, KT, 2 + 2 * RB], f32, S0 + 41632)
    last_o = at("conv_last_rows", [2 + 2 * RB, D], f32, S0 + 42208)
    ppT = at("ple_projT", [P, KT, T], f32, S0 + 20480)
    sgm = at("ple_gate", [P, 2, T], f32, S0)
    o_sb = at("y_rows", [P, 2, D], f32, S0)

    def xh(name, shape, dt, off):
        n = 4
        for s in shape[1:]:
            n *= s
        assert XH0 + off + n <= XH1, name
        return at(name, shape, dt, XH0 + off)

    lnp = xh("ln_params", [P, 2, D], f32, 0)
    p_tok = xh("p_tok", [P, NT, PLE], f32, 8192)
    pThi = xh("pT_hi", [P, 2, T], f32r, 13312)
    pTlo = xh("pT_lo", [P, 2, T], f32r, 17920)
    x1T = [xh("x1T_0", [P, KT, P], f32, 22528), at("x1T_1", [P, KT, P], f32, S0 + 38912)]
    wr = xh("w_router", [P, KT, 20], f32, 26624)
    br = xh("b_router", [P, 20], f32, 27264)
    rt = xh("routing", [P, 1120], f32, 27648)
    roff = [0]

    def rtile(*shape):
        n = 1
        for s in shape:
            n *= s
        a = rt[:, roff[0]:roff[0] + n]
        roff[0] += n
        if len(shape) == 2:
            a = a.rearrange("p (a b) -> p a b", b=shape[1])
        if len(shape) == 3:
            a = a.rearrange("p (a b c) -> p a b c", b=shape[1], c=shape[2])
        return a

    lg = rtile(NT, 20)
    r4 = rtile(NT, 4)
    ohg = rtile(NT, 4)
    oh1 = rtile(NT, 4)
    oh2 = rtile(NT, 4)
    ein = rtile(NT, 4)
    s5 = rtile(8, NT)
    m16 = rtile(NT, NE)
    oh16 = [rtile(NT, 4, 4), rtile(NT, 4, 4)]
    t16 = rtile(NT, 4, 4)
    post = rtile(NT, NE)
    ovw = rtile(6, 24)
    wide = rtile(OVF, NE)
    pmd = rtile(3, 2 * NT)
    mpre = rtile(NT + 1, NE)
    amat = xh("slot_onehot", [P, 2, P], f32, 32512)
    bmat = xh("tile_onehot", [P, 2, SLOT_TILES], f32, 33536)
    posi = xh("pos_int", [P, 3, 2 * NT], i32, 33728)
    xg = xh("x_gathered", [P, 2, D], f32, 0)
    eTh = xh("xgT_hi", [P, D], f32r, 8192)
    eTl = xh("xgT_lo", [P, D], f32r, 12288)
    act_a = xh("expert_act", [P, 2, F], f32, 16384)
    aTh = xh("expert_actT_hi", [P, F], f32r, 18432)
    aTl = xh("expert_actT_lo", [P, F], f32r, 19456)
    y_sb = xh("expert_y", [P, D], f32, 20480)
    eTf = xh("xgT_full", [P, D], f32, 24576)
    aTf = xh("expert_actT_full", [P, F], f32, 28672)
    yg = xh("y_gathered", [P, 3, 2, D], f32, 8192)
    yg3 = at("y_gathered3", [P, 2, D], f32, S0 + 38912)

    def yrows(i, n, k):
        return yg3[0:n, k, :] if i % 4 == 3 else yg[0:n, i % 4, k, :]


    ctx = ExitStack()
    with ctx:
        ps = ctx.enter_context(nc.psum_tensor("ps", [P, 8, 512], f32))

        def sem(name):
            return ctx.enter_context(nc.semaphore(name))

        wld = [sem(f"w_loaded{j}") for j in range(4)]
        x_ld, small_ld, ws_ld, bv_ld = sem("x_loaded"), sem("small_loaded"), sem("ws_loaded"), sem("v_bias_loaded")
        blk_ld, bsl_ld = sem("blocks_loaded"), sem("bias_low_loaded")
        vc_ld, ln_ld, p_ld, wr_ld, past_ld = sem("v_cols_loaded"), sem("ln_loaded"), sem("p_loaded"), sem("router_loaded"), sem("past_loaded")
        xg_ld = [sem("x_gathered0"), sem("x_gathered1")]
        yg_ld = [sem(f"y_gathered{j}") for j in range(4)]
        ov_ld, ovx_ld = [sem("ovf_w0"), sem("ovf_w1")], [sem("ovf_x0"), sem("ovf_x1")]
        hi_done, split_done = sem("w_hi_done"), sem("w_split_done")
        eu_used = sem("expert_unit_used")
        mt_done = sem("pair_done")
        const_ok, cols_ok, ws_t, ws_cp, ws_ok = sem("consts_ready"), sem("cols_ready"), sem("ws_turned"), sem("ws_copied"), sem("ws_ready")
        bs_ok, bsh_ok, bsl_ok, ones_ok = sem("bias_spread"), sem("bias_high"), sem("bias_low"), sem("ones_ready")
        tr_done, tr_free = sem("turned"), sem("turned_free")
        xT_ok, xhi_ok, xlo_ok = sem("xT_ready"), sem("xhi_ready"), sem("xlo_ready")
        vps_done, vz_done, vg_done, vs_done, v_st = sem("v_product"), sem("v_biased"), sem("v_gelu"), sem("v_stats_done"), [sem("v_stored0"), sem("v_stored1")]
        vn_ok, vstate_st, sg_done, gm_done = sem("v_normed"), sem("v_state_stored"), sem("gate_product"), sem("g_done")
        u_done, gh_done, gl_done = sem("u_done"), sem("g_hi_done"), sem("g_lo_done")
        o_done = sem("out_added")
        pp_done = sem("ple_proj_copied")
        st_ok, sq_ok, rs_ok, nz_ok, ng_ok, nb_ok = sem("stats_ready"), sem("std_ready"), sem("rstd_ready"), sem("normed"), sem("norm_scaled"), sem("norm_done")
        x_st = sem("x_stored")
        p_turn, ph_ok, pl_ok = sem("p_turned"), sem("pT_hi_ready"), sem("pT_lo_ready")
        r_turn, r_cp, r_mm = sem("router_turned"), sem("router_copied"), sem("router_product")
        r_ex, r_ex_ok, m_ok, rank_ok, ab_ok, ab_used, idx_ok = sem("exp_asked"), sem("exp_ready"), sem("onehot_ready"), sem("rank_ready"), sem("slot_onehot_ready"), sem("slot_onehot_used"), sem("idx_ready")
        xs_ok, ym_ok, cb_ok = sem("x_scaled"), sem("first_rows_weighted"), sem("first_rows_added")
        xtp, eth_ok, etl_ok = sem("xg_turned"), sem("xgT_hi_ready"), sem("xgT_lo_ready")
        si_ok, a_ok, at_ok, ath_ok, atl_ok = sem("silu_done"), sem("a_ready"), sem("a_turned"), sem("aT_hi_ready"), sem("aT_lo_ready")
        y_cp, y_st = sem("y_copied"), sem("y_stored")
        ov = [{n: sem(f"ovf_{n}{l}") for n in ("turned", "copied", "gu", "silu", "a", "aturned", "acopied", "y", "ycopied", "stored")} for l in range(DEPTH)]
        sg_ok, pe_ok = sem("gate_ready"), sem("layer_done")
        c_ok, cx_ok = sem("c_copied"), sem("cx_ready")
        past_t, last_ok, last_t, last_cp, cs_st = sem("past_turned"), sem("last_ready"), sem("last_turned"), sem("last_copied"), sem("conv_state_stored")
        out_cp, out_st = sem("rows_copied"), [sem("rows_stored0"), sem("rows_stored1")]
        dch, pch = sem("vector_chain"), sem("pool_chain")

        block = ctx.enter_context(nc.Block())

        def tok(i):
            return P if i < NT - 1 else TS

        def w8(w, j, k, c0, n=P):
            return w[:, j, k * 256 + c0:k * 256 + c0 + n]

        def w4(w, j, k, c0, n=P):
            return w[:, j, k * 512 + c0:k * 512 + c0 + n]

        def xk(x, k, c0, n):
            return x[:, k * T + c0:k * T + c0 + n]

        def pair(par):
            return ps[:, 2 * par:2 * par + 2, 0:HALF]

        def halves(a):
            return a.rearrange("p (h t) -> p h t", h=2)

        def turned_bank(n):
            return 4 + 2 * (n % 2)

        def loads_of_slot(d):
            return 16 * (d // 4 + 1)

        def gu_unit(s):
            return 3 * s - 1 if s else 0

        def dn_unit(s):
            return 3 * s + 4 if s < NE - 1 else EU - 1

        def tiles_through(d):
            if d < U_P[0]:
                r, j = divmod(d - U_A, 4)
                return M_A + 12 * r + (2, 4, 8, 12)[j]
            if U_B <= d < U_P[1]:
                r, j = divmod(d - U_B, 4)
                return M_B + 12 * r + (2, 4, 8, 12)[j]
            for u0, m0 in ((U_G[1], M_G[1]), (U_P[1], M_P[1]), (U_CH, M_CH), (U_G[0], M_G[0]), (U_P[0], M_P[0])):
                if d >= u0:
                    return m0 + 2 * (d - u0 + 1)

        def wait_used(eng, d, it=0, step=0):
            for l in range(DEPTH):
                if U_E[l] + 4 <= d < U_G[l] + 4:
                    eng.wait_ge(eu_used, it * step + (EU * l + d - U_E[l] - 3))
                    return
            if d - 4 >= U_A:
                eng.wait_ge(mt_done, it * (3 * step) + tiles_through(d - 4))
            elif d >= 4:
                eng.wait_ge(vps_done, it * (NT * step) + NT * (d - 3))

        TR_IN = 0
        TR_N1 = [NT, NT * 3]
        TR_N2 = [NT * 2, NT * 4]
        TR_OUT = NT * 5
        TF_N2 = [NT, NT * 2]
        V_DONE = NT * VU

        @block.sync
        def _(sp):
            nc.allow_non_contiguous_dma(reason="rows of weight units")

            def load_unit(d, j, src, n=UNIT, shape=None, it=None, wait=None):
                if wait is not None:
                    sp.wait_ge(split_done, wait)
                sp.dma_start(raw[:, j, 0:n] if shape is None else raw[:, j, 0:n].rearrange("p (k c) -> p k c", c=shape),
                             src).then_inc(wld[j], 16)

            def cols8(w, c0):
                return w[:, ds(c0, 256)].rearrange("(k p) c -> p k c", p=P)

            def rows4(w, r0, c0):
                return w[ds(r0, 512), c0:c0 + 512].rearrange("(k p) c -> p k c", p=P)

            sp.dma_start(xtok[:, 0:4, :], x_prompt).then_inc(x_ld, 16)
            sp.dma_start(xtok[0:TS, 4, :], x_sample).then_inc(x_ld, 16)
            for j in range(4):
                load_unit(j, j, cols8(w_in, AW + 256 * j), shape=256)
            with sp.Fori(1, VU // 4) as it:
                for j in range(4):
                    load_unit(0, j, cols8(w_in, it * 1024 + (AW + 256 * j)), shape=256, wait=it * 4 + (U_V + j - 3))
            with sp.Fori(0, AR) as it:
                for j in range(2):
                    load_unit(0, j, cols8(w_in, it * 512 + 256 * j), shape=256, wait=it * 4 + (U_A + j - 3))
                for j in range(2):
                    load_unit(0, 2 + j, rows4(w_out, it * 512, 512 * j), shape=512, wait=it * 4 + (U_A + 2 + j - 3))
            for l in range(DEPTH):
                for j in range(4):
                    load_unit(0, j, x_in["ple_w_proj"][l][:, 256 * j:256 * j + 256].rearrange("(k p) c -> p k c", p=P),
                              n=512, shape=256, wait=U_P[l] + j - 3)
                g_src, d_src = x_in["moe_w_gate_up"][l], x_in["moe_w_down"][l]

                def expert_load(e, src, width, it=None):
                    d = U_E[l] + e
                    sp.wait_ge(split_done, d - 3 if it is None else it * 12 + (d - 3))
                    sp.dma_start(raw[:, e % 4, :].rearrange("p (k c) -> p k c", c=width), src).then_inc(wld[e % 4], 16)

                def load_step(s, it=None):
                    at_ = s if it is None else it * 4 + s
                    if s < NE:
                        for a in range(2):
                            expert_load(gu_unit(s) + a, g_src[at_, 512 * a:512 * a + 512, :].rearrange("(k p) c -> p k c", p=P), 2 * F, it)
                    if s:
                        expert_load(dn_unit(s - 1), d_src[at_ - 1, :, :].rearrange("(k p) c -> p k c", p=P), D, it)

                load_step(0)
                load_step(1)
                with sp.Fori(0, 3) as it:
                    for s in range(2, 6):
                        load_step(s, it)
                for s in range(NE - 2, NE + 1):
                    load_step(s)
                sp.wait_ge(idx_ok, 3 * (l + 1))
                n = sp.value_load(n_ovf[0:1, 0:1], min_val=0, max_val=OVF)
                with sp.If(n > 0):
                    sp.wait_ge(split_done, U_G[l])

                    def ovf_load(i):
                        e = sp.value_load(ovf_e[0:1, ds(i, 1)], min_val=0, max_val=NE - 1)
                        for a in range(2):
                            sp.dma_start(raw[:, a, :].rearrange("p (k c) -> p k c", c=2 * F),
                                         g_src[ds(e, 1), 512 * a:512 * a + 512, :].rearrange("e (k p) c -> p (e k) c", p=P)).then_inc(ov_ld[l], 16)
                        sp.dma_start(raw[:, 2, :].rearrange("p (k c) -> p k c", c=D),
                                     d_src[ds(e, 1), :, :].rearrange("e (k p) c -> p (e k) c", p=P)).then_inc(ov_ld[l], 16)

                    ovf_load(0)
                    with sp.Fori(1, OVF) as i:
                        sp.wait_ge(ov[l]["y"], i)
                        ovf_load(i)
                    sp.wait_ge(ov[l]["y"], OVF)
                for j in range(4):
                    load_unit(0, j, cols8(x_in["ple_w_gate"][l], 256 * j), shape=256, wait=U_G[l] + j - 3)
                if l == 0:
                    with sp.Fori(0, 2) as it:
                        for j in range(4):
                            load_unit(0, j, cols8(bw_in, it * 512 + (D * (1 + j % 2) + 256 * (j // 2))), shape=256,
                                      wait=it * 4 + (U_CH + j - 3))
                    with sp.Fori(0, BR) as it:
                        for j in range(2):
                            load_unit(0, j, cols8(bw_in, it * 512 + 256 * j), shape=256, wait=it * 4 + (U_B + j - 3))
                        for j in range(2):
                            load_unit(0, 2 + j, rows4(bw_out, it * 512, 512 * j), shape=512, wait=it * 4 + (U_B + 2 + j - 3))
            for i in range(NT):
                sp.wait_ge(out_cp, i + 1)
                dst = y_prompt[:, i, :] if i < 4 else y_sample
                sp.dma_start(dst, o_sb[0:tok(i), i % 2, :]).then_inc(out_st[i % 2], 16)
            sp.wait_ge(out_st[0], 48)
            sp.wait_ge(out_st[1], 32)

        @block.gpsimd
        def _(pool):
            ch = Chain(pool, pch)
            pool.dma_start(colsrc[0:24, :], x_in["a_b_in"][0, 0:AW].rearrange("(f p) -> f p", p=P)).then_inc(small_ld, 16)
            pool.dma_start(colsrc[24:40, :], x_in["ple_b_gate"].rearrange("l (f p) -> (l f) p", p=P)).then_inc(small_ld, 16)
            pool.dma_start(colsrc[40:64, :], x_in["b_conv_w"][0].rearrange("w (f p) -> (w f) p", p=P)).then_inc(small_ld, 16)
            pool.dma_start(colsrc[64:80, :], x_in["ln2_g"].rearrange("l (f p) -> (l f) p", p=P)).then_inc(small_ld, 16)
            pool.dma_start(colsrc[80:96, :], x_in["ln2_b"].rearrange("l (f p) -> (l f) p", p=P)).then_inc(small_ld, 16)
            pool.dma_start(wsrc[:, :, :], x_in["a_w_s"][0].rearrange("h t s -> t h s")).then_inc(ws_ld, 16)
            pool.dma_start(bsrc[:, :, :], x_in["a_b_s"]).then_inc(ws_ld, 16)
            pool.dma_start(bvb[:, :], x_in["a_b_in"][0:1, AW:2 * AW].to_broadcast([P, AW])).then_inc(bv_ld, 16)
            ch.link(pool.memset(ident[:, :], 0.0))
            pool.memset(ones[:, :], 1.0)
            pool.memset(below[:, :], 1.0)
            pool.memset(eps[:, :], EPS)
            ch.link(pool.memset(xT[:, KT * T:], 0.0))
            ch.link(pool.memset(xtok[TS:P, 4, :], 0.0))
            ch.link(pool.memset(wss[:, :, :], 0.0))
            pool.affine_select(out=ident[:, :], in_=ident[:, :], compare_op=ALU.not_equal, fill=1.0, base=0,
                               pattern=[[-1, P]], channel_multiplier=1)
            pool.affine_select(out=below[:, :], in_=below[:, :], compare_op=ALU.is_gt, fill=0.0, base=0,
                               pattern=[[1, P]], channel_multiplier=-1)
            pool.iota(iota[:, :], pattern=[[1, P]], base=0, channel_multiplier=0, allow_small_or_imprecise_dtypes=True)
            pool.iota(iota_e[:, :], pattern=[[P, NE]], base=0, channel_multiplier=0, allow_small_or_imprecise_dtypes=True)
            ch.link(pool.iota(tokid[:, :], pattern=[[P, NT]], base=0, channel_multiplier=1, allow_small_or_imprecise_dtypes=True))
            pool.memset(tokid[TS:P, 4:5], 0.0).then_inc(const_ok, 1)
            pool.wait_ge(ws_cp, 1)
            pool.affine_select(out=wst[:, :, :], in_=wst[:, :, :], compare_op=ALU.is_ge, fill=0.0, base=0,
                               pattern=[[0, NH], [1, P]], channel_multiplier=-1).then_inc(ws_ok, 1)
            pool.wait_ge(ws_ok, 1)
            for b in range(RB):
                pool.dma_start(wss[SB * b:SB * b + SB, :, SB * b:SB * b + SB], wst[0:SB, :, 0:SB]).then_inc(blk_ld, 16)
            pool.wait_ge(bsl_ok, 1)
            pool.dma_start(bsx[1:2, :, :], bsl[:, :, :]).then_inc(bsl_ld, 16)
            def v_store(it):
                for j in range(2):
                    pool.wait_ge(vg_done, it * (2 * NT) + NT * (j + 1))
                    dst = v_dram[:, :, ds(it * 512 + 256 * j, 256)]
                    pool.dma_start(dst[0:4].rearrange("i p c -> p i c"), vst[:, j, 0:4, :]).then_inc(v_st[j], 16)
                    pool.dma_start(dst[4, 0:TS, :], vst[0:TS, j, 4, :]).then_inc(v_st[j], 16)

            def vrows(r):
                pool.dma_start(vc[:, 0:4, :], v_dram[0:4, :, ds(r * 512, 512)].rearrange("i p c -> p i c")).then_inc(vc_ld, 16)
                pool.dma_start(vc[0:TS, 4, :], v_dram[4, 0:TS, ds(r * 512, 512)]).then_inc(vc_ld, 16)

            def vparams(r):
                for n, name in enumerate(("a_ln_g", "a_ln_b")):
                    pool.dma_start(gb[:, n, :], x_in[name][0:1, ds(r * 512, 512)].to_broadcast([P, 512])).then_inc(vc_ld, 16)

            def vstate(r):
                pool.dma_start(v_state_p[:, ds(r * 512, 512)], vc[:, 3, :]).then_inc(vstate_st, 16)
                pool.dma_start(v_state_s[:, ds(r * 512, 512)], vc[0:TS, 4, :]).then_inc(vstate_st, 16)

            v_store(0)
            pool.wait_ge(v_st[0], 32)
            pool.wait_ge(v_st[1], 32)
            vrows(0)
            with pool.Fori(1, VU // 2) as it:
                v_store(it)
            pool.wait_ge(vz_done, V_DONE)
            vparams(0)
            pool.wait_ge(v_st[0], VU // 2 * 32)
            pool.wait_ge(v_st[1], VU // 2 * 32)
            with pool.Fori(0, AR - 1) as r:
                pool.wait_ge(vn_ok, r * NT + NT)
                vstate(r)
                pool.wait_ge(vstate_st, r * 32 + 32)
                pool.wait_ge(sg_done, r * ROUND + ROUND)
                vrows(r + 1)
                vparams(r + 1)
            pool.wait_ge(vn_ok, AR * NT)
            vstate(AR - 1)
            pool.wait_ge(vstate_st, AR * 32)

            for l in range(DEPTH):
                pool.wait_ge(mt_done, M_P[l] - KT)
                for n, g in enumerate((x_in["ln1_g"], x_in["ln1_b"])):
                    pool.dma_start(lnp[:, n, :], g[l:l + 1, :].to_broadcast([P, D])).then_inc(ln_ld, 16)
                pool.dma_start(p_tok[:, 0:4, :], x_in["p_prompt"][l, 0].rearrange("(i p) d -> p i d", p=P)).then_inc(p_ld, 16)
                pool.dma_start(p_tok[0:TS, 4, :], x_in["p_sample"][l].rearrange("b s d -> (b s) d")).then_inc(p_ld, 16)
                pool.dma_start(wr[:, :, 0:4], x_in["moe_w_group"][l].rearrange("(k p) c -> p k c", p=P)).then_inc(wr_ld, 16)
                pool.dma_start(wr[:, :, 4:20], x_in["moe_w_expert"][l].rearrange("(k p) c -> p k c", p=P)).then_inc(wr_ld, 16)
                pool.dma_start(br[:, 0:4], x_in["moe_b_group"][l:l + 1, :].to_broadcast([P, 4])).then_inc(wr_ld, 16)
                pool.dma_start(br[:, 4:20], x_in["moe_b_expert"][l:l + 1, :].to_broadcast([P, 16])).then_inc(wr_ld, 16)
                for i in range(NT):
                    pool.wait_ge(ng_ok, NT * l + i + 1)
                    pool.tensor_tensor(xtok[:, i, :], xtok[:, i, :], lnp[:, 1, :], ALU.add).then_inc(nb_ok, 1)
                    pool.wait_ge(nb_ok, NT * l + i + 1)
                    pool.dma_start(x_dram[l][P * i:P * i + tok(i), :], xtok[0:tok(i), i, :]).then_inc(x_st, 16)
                pool.wait_ge(x_st, 16 * NT * (l + 1))
                pool.wait_ge(idx_ok, 3 * (l + 1))

                def gather(s):
                    if s >= 2:
                        pool.wait_ge(xtp, 2 * (NE * l + s - 1))
                    pool.indirect_dma_start(out=xg[:, s % 2, :], out_offset=None, in_=x_dram[l][:, :],
                                            in_offset=bass.IndirectOffsetOnAxis(ap=idx[:, s:s + 1], axis=0)).then_inc(xg_ld[s % 2], 16)

                for s in range(NE):
                    gather(s)
                n = pool.value_load(n_ovf[0:1, 0:1], min_val=0, max_val=OVF)
                with pool.If(n > 0):
                    o = ov[l]
                    pool.wait_ge(xtp, 2 * NE * (l + 1))
                    for i in range(OVF):
                        if i:
                            pool.wait_ge(o["turned"], i)
                        pool.indirect_dma_start(out=xg[:, 0, :], out_offset=None, in_=x_dram[l][:, :],
                                                in_offset=bass.IndirectOffsetOnAxis(ap=idx[:, NE + i:NE + i + 1], axis=0)).then_inc(ovx_ld[l], 16)
                    pool.wait_ge(o["stored"], 16 * OVF)
                pool.wait_ge(y_st, 16 * NE * (l + 1))
                pool.wait_ge(etl_ok, 2 * NE * (l + 1))
                pool.wait_ge(eu_used, EU * (l + 1))

                def norm2(rows):
                    for i in range(NT):
                        if i >= 4:
                            pool.wait_ge(st_ok, 2 * NT * l + NT + i - 3)
                        for k in range(2):
                            pool.indirect_dma_start(out=yrows(i, tok(i), k), out_offset=None, in_=y_dram[l][0:rows, :],
                                                    in_offset=bass.IndirectOffsetOnAxis(ap=pos_u[0:tok(i), i, k:k + 1], axis=0)).then_inc(yg_ld[i % 4], 16)
                    pool.wait_ge(xs_ok, l + 1)
                    for i in range(3, NT):
                        t = tok(i)
                        pool.wait_ge(ym_ok, 2 * l + i - 2)
                        pool.tensor_tensor(xtok[0:t, i, :], xtok[0:t, i, :], yrows(i, t, 0), ALU.add).then_inc(cb_ok, 1)

                with pool.If(n > 0):
                    norm2(SLOT_TILES * CAP)
                with pool.If(n < 1):
                    norm2(NE * CAP)
                if l == 0:
                    pool.wait_ge(pe_ok, KT)
                    pool.dma_start(past[:, :], x_in["state_conv"][0].rearrange("b w d -> (b w) d")).then_inc(past_ld, 16)
                    pool.wait_ge(last_cp, 1)
                    pool.dma_start(conv_state_p, last_o[0:2, :]).then_inc(cs_st, 16)
                    pool.dma_start(conv_state_s, last_o[2:18, :]).then_inc(cs_st, 16)
                    pool.wait_ge(cs_st, 32)

        @block.scalar
        def _(act):
            def hi(d, it=0, step=0):
                j = d % 4
                n = 512 if U_P[0] <= d < U_E[0] or U_P[1] <= d < U_E[1] else UNIT
                assert step % 4 == 0
                act.wait_ge(wld[j], it * (4 * step) + loads_of_slot(d))
                wait_used(act, d, it, step)
                act.activation(whi[:, j, 0:n], raw[:, j, 0:n], ACT.Copy).then_inc(hi_done, 1)

            for i in range(NT):
                act.wait_ge(tr_done, TR_IN + i + 1)
                b = turned_bank(TR_IN + i)
                src = ps[:, b:b + 2, :].rearrange("p b (k t) -> p (b k) t", t=P)[:, :, 0:tok(i)]
                dst = xT[:, 0:KT * T].rearrange("p (k t) -> p k t", t=T)[:, :, P * i:P * i + tok(i)]
                act.activation(dst, src, ACT.Copy).then_inc(tr_free, 1)
                act.wait_ge(tr_free, TR_IN + i + 1)
                act.activation(xhi[:, 0:KT * T].rearrange("p (k t) -> p k t", t=T)[:, :, P * i:P * i + tok(i)], dst,
                               ACT.Copy).then_inc(xhi_ok, 1)
                if i == 1:
                    hi(0)
            act.activation(xhi[:, KT * T:], xT[:, KT * T:], ACT.Copy).then_inc(xhi_ok, 1)
            for d in range(1, 4):
                hi(d)
            act.wait_ge(bs_ok, 1)
            act.activation(bsx[0:1, :, :], bss[:, :, :], ACT.Copy).then_inc(bsh_ok, 1)
            act.wait_ge(const_ok, 1)
            act.activation(ones_r[:, :], ones[:, :], ACT.Copy).then_inc(ones_ok, 1)

            def v_unit(n, it=0, step=0):
                for i in range(NT):
                    act.wait_ge(vz_done, it * (NT * step) + (NT * n + i + 1))
                    act.activation(vst[:, n % 2, i, :], vst[:, n % 2, i, :], ACT.Gelu).then_inc(vg_done, 1)
                    if i == 1 and n + AHEAD >= 4:
                        hi(n + AHEAD, it, step)

            for n in range(2):
                v_unit(n)
            with act.Fori(0, (VU - 4) // 4) as it:
                for j in range(4):
                    v_unit(2 + j, it, 4)
            for n in (VU - 2, VU - 1):
                v_unit(n)
            act.wait_ge(rs_ok, 1)
            act.activation(rstd[:, :], rstd[:, :], ACT.Sqrt).then_inc(sq_ok, 1)

            def a_round(r, it, step, split):
                for fl in range(ROUND):
                    act.wait_ge(gl_done, it * (ROUND * step) + (ROUND * r + fl - 1)) if (r or step or fl >= 2) else None
                    act.wait_ge(mt_done, it * (12 * step) + (M_A + 12 * r + fl + 1))
                    act.wait_ge(cols_ok, 1)
                    act.activation(halves(gf[:, fl % 2, :]), pair(fl % 2), ACT.Gelu,
                                   bias=cols[:, ds(it * (ROUND * step) + (C_BU + ROUND * r + fl), 1)]).then_inc(u_done, 1)
                    if fl % 2 == 0:
                        split(fl // 2)
                    act.wait_ge(gm_done, it * (ROUND * step) + (ROUND * r + fl + 1))
                    act.activation(ghi[:, fl, :], gf[:, fl % 2, :], ACT.Copy).then_inc(gh_done, 1)
                split(2)
                split(3)

            a_round(0, 0, 0, lambda j: hi(U_A + j + AHEAD))
            with act.Fori(0, AR - 2) as it:
                a_round(1, it, 1, lambda j: hi(U_A + 4 + j + AHEAD, it, 4))
            a_round(AR - 1, 0, 0, lambda j: hi(U_P[0] - 4 + j + AHEAD))

            def norm_tile(l, which, i):
                n = 2 * NT * l + NT * which + i
                act.wait_ge(st_ok, n + 1)
                act.activation(rstd[:, i:i + 1], mv[:, i, 1:2], ACT.Sqrt, bias=eps[:, 0:1]).then_inc(sq_ok, 1)
                act.wait_ge(rs_ok, 1 + n + 1)
                if which == 0:
                    b = turned_bank(TR_N1[l] + i)
                    dst, src = xtok[:, i, :].rearrange("p (b t) -> p b t", b=2), ps[:, b:b + 2, :]
                else:
                    dst, src = xtok[:, i, :], xtok[:, i, :]
                act.activation(dst, src, ACT.Identity, bias=nmr[:, i:i + 1], scale=rstd[:, i:i + 1]).then_inc(nz_ok, 1)

            for l in range(DEPTH):
                norm_tile(l, 0, 0)
                norm_tile(l, 0, 1)
                for i in range(NT):
                    act.wait_ge(p_turn, NT * l + i + 1)
                    act.activation(pThi[:, :, P * i:P * i + tok(i)],
                                   ps[:, i % 4, 0:2 * P].rearrange("p (k t) -> p k t", t=P)[:, :, 0:tok(i)], ACT.Copy).then_inc(ph_ok, 1)
                hi(U_P[l] + AHEAD)

                def proj_out(mo):
                    act.wait_ge(mt_done, M_P[l] + mo + 1)
                    act.activation(halves(ppT[:, mo, :]), pair(mo % 2), ACT.Copy).then_inc(pp_done, 1)

                def router_rows(i):
                    act.wait_ge(r_turn, NT * l + i + 1)
                    if i >= 2:
                        act.wait_ge(r_mm, NT * l + i - 1)
                    act.activation(x1T[i % 2][:, :, :].rearrange("p (b k) t -> p b (k t)", b=2), ps[:, 2:4, :],
                                   ACT.Copy).then_inc(r_cp, 1)

                proj_out(0)
                proj_out(1)
                norm_tile(l, 0, 2)
                proj_out(2)
                proj_out(3)
                norm_tile(l, 0, 3)
                norm_tile(l, 0, 4)
                for i in range(NT):
                    router_rows(i)
                    if 1 <= i < 3:
                        hi(U_E[l] + i - 1)
                proj_out(4)
                proj_out(5)
                act.wait_ge(r_ex, 2 * l + 1)
                act.activation(r4[:, :, :], r4[:, :, :], ACT.Exp).then_inc(r_ex_ok, 1)
                act.wait_ge(r_ex, 2 * l + 2)
                act.activation(s5[:, 3, :], s5[:, 3, :], ACT.Exp).then_inc(r_ex_ok, 1)
                proj_out(6)
                proj_out(7)

                def xT_hi(s, it=0, step=0):
                    q = it * (2 * step) + 2 * (NE * l + s)
                    for b in range(2):
                        act.wait_ge(xtp, q + (b + 1))
                        act.activation(eTh[:, 512 * b:512 * b + 512], ps[:, 2 + b, :], ACT.Copy).then_inc(eth_ok, 1)

                def y_out(s, it=0, step=0):
                    q = it * step + (NE * l + s)
                    act.wait_ge(eu_used, it * (3 * step) + (EU * l + dn_unit(s) + 1))
                    if l or s or step:
                        act.wait_ge(y_st, q * 16)
                    act.activation(y_sb[:, :].rearrange("p (b t) -> p b t", b=2), ps[:, 4:6, :], ACT.Copy).then_inc(y_cp, 1)
                    act.wait_ge(y_cp, q + 1)
                    act.dma_start(y_dram[l][ds(it * (P * step) + P * s, P), :], y_sb[:, :]).then_inc(y_st, 16)

                def expert_hi(e, it, step):
                    if e < EU:
                        hi(U_E[l] + e, it, 3 * step)

                def moe_step(s, it=0, step=0):
                    e = 3 * s + 2
                    expert_hi(e, it, step)
                    expert_hi(e + 1, it, step)
                    if s < NE:
                        q = it * step + (NE * l + s)
                        act.wait_ge(eu_used, it * (3 * step) + (EU * l + gu_unit(s) + 2))
                        act.activation(act_a[:, 0, :], ps[:, 0, 0:F], ACT.Silu).then_inc(si_ok, 1)
                    if s < NE - 1:
                        xT_hi(s + 1, it, step)
                        expert_hi(e + 2, it, step)
                    if s >= 1:
                        y_out(s - 1, it, step)
                    if s < NE:
                        act.wait_ge(at_ok, q + 1)
                        act.activation(aTh[:, :], ps[:, 1, 0:F], ACT.Copy).then_inc(ath_ok, 1)

                act.wait_ge(x_st, 16 * NT * (l + 1))
                act.activation(xtok[:, :, :], xtok[:, :, :], ACT.Copy, scale=ALPHA).then_inc(xs_ok, 1)
                xT_hi(0)
                moe_step(0)
                moe_step(1)
                with act.Fori(0, 3) as it:
                    for s in range(2, 6):
                        moe_step(s, it, 4)
                for s in range(NE - 2, NE + 1):
                    moe_step(s)
                act.wait_ge(idx_ok, 3 * (l + 1))
                n = act.value_load(n_ovf[0:1, 0:1], min_val=0, max_val=OVF)
                with act.If(n > 0):
                    o = ov[l]
                    act.wait_ge(y_st, 16 * NE * (l + 1))
                    with act.Fori(0, OVF) as i:
                        act.wait_ge(o["turned"], i + 1)
                        act.activation(eTf[:, :].rearrange("p (b t) -> p b t", b=2), ps[:, 2:4, :], ACT.Copy).then_inc(o["copied"], 1)
                        act.wait_ge(o["gu"], i + 1)
                        act.activation(act_a[:, 0, :], ps[:, 0, 0:F], ACT.Silu).then_inc(o["silu"], 1)
                        act.wait_ge(o["aturned"], i + 1)
                        act.activation(aTf[:, :], ps[:, 1, 0:F], ACT.Copy).then_inc(o["acopied"], 1)
                        act.wait_ge(o["y"], i + 1)
                        act.activation(y_sb[:, :].rearrange("p (b t) -> p b t", b=2), ps[:, 4:6, :], ACT.Copy).then_inc(o["ycopied"], 1)
                        act.wait_ge(o["ycopied"], i + 1)
                        act.dma_start(y_dram[l][ds(i * P + NE * P, P), :], y_sb[:, :]).then_inc(o["stored"], 16)
                        act.wait_ge(o["stored"], i * 16 + 16)
                for j in range(AHEAD):
                    hi(U_G[l] + j)

                def n2_cols(i):
                    b = turned_bank(TR_N2[l] + i)
                    act.wait_ge(tr_done, TR_N2[l] + i + 1)
                    src = ps[:, b:b + 2, :].rearrange("p b (k t) -> p (b k) t", t=P)[:, :, 0:tok(i)]
                    act.activation(xT[:, 0:KT * T].rearrange("p (k t) -> p k t", t=T)[:, :, P * i:P * i + tok(i)], src,
                                   ACT.Copy).then_inc(tr_free, 1)

                def weigh(i):
                    act.wait_ge(yg_ld[i % 4], 32 * ((2 if i % 4 == 0 else 1) * l + i // 4 + 1))
                    y = yrows(i, tok(i), 0)
                    act.activation(y, y, ACT.Copy, scale=wtop[0:tok(i), 0, i:i + 1]).then_inc(ym_ok, 1)

                for i in range(NT):
                    norm_tile(l, 1, i)
                    if i < 2:
                        weigh(i + 3)
                    if i:
                        n2_cols(i - 1)
                n2_cols(NT - 1)

                def x_hi(wait_sem, value):
                    act.wait_ge(wait_sem, value)
                    for k in range(KT):
                        if wait_sem is xT_ok:
                            act.wait_ge(xT_ok, value + k)
                        act.activation(xk(xhi, k, 0, T), xk(xT, k, 0, T), ACT.Copy).then_inc(xhi_ok, 1)

                x_hi(xT_ok, KT * l + 1)
                for j in range(4):
                    if U_G[l] + j + AHEAD < U_END:
                        hi(U_G[l] + j + AHEAD)
                    for m in range(2):
                        mo = 2 * j + m
                        act.wait_ge(mt_done, M_G[l] + mo + 1)
                        if mo >= 2:
                            act.wait_ge(pe_ok, KT * l + mo - 1)
                        act.activation(halves(sgm[:, m, :]), pair(m), ACT.Sigmoid,
                                       bias=cols[:, C_BG + KT * l + mo:C_BG + KT * l + mo + 1]).then_inc(sg_ok, 1)
                if l == 0:
                    act.wait_ge(mt_done, M_G[0] + KT)
                    x_hi(pe_ok, KT)

                    for jj in range(4):
                        for m in range(2):
                            act.wait_ge(mt_done, M_CH + 4 * jj + m + 1)
                            if jj:
                                act.wait_ge(cx_ok, 2 * jj - 1 + m)
                            act.activation(halves(c_sb[:, m, :]), pair(m), ACT.Copy).then_inc(c_ok, 1)
                        hi(U_CH + 2 * jj + AHEAD)
                        hi(U_CH + 2 * jj + 1 + AHEAD)
                    for r in range(BR):
                        for fl in range(ROUND):
                            q = ROUND * (AR + r) + fl
                            act.wait_ge(gm_done, q + 1)
                            act.activation(ghi[:, fl, :], gf[:, fl % 2, :], ACT.Copy).then_inc(gh_done, 1)
                            hi(U_B + 4 * r + fl + AHEAD)
                        if r == 0:
                            act.wait_ge(last_t, 1)
                            act.activation(last_o[:, :].rearrange("p (b t) -> p b t", b=2), ps[0:18, 6:8, :],
                                           ACT.Copy).then_inc(last_cp, 1)
            for i in range(NT):
                b = turned_bank(TR_OUT + i)
                act.wait_ge(tr_done, TR_OUT + i + 1)
                if i >= 2:
                    act.wait_ge(out_st[i % 2], 16 * (i // 2))
                act.activation(o_sb[:, i % 2, :].rearrange("p (b t) -> p b t", b=2), ps[:, b:b + 2, :],
                               ACT.Copy).then_inc(out_cp, 1)

        @block.vector
        def _(dve):
            ch = Chain(dve, dch)

            def lo(d, it=0, step=0):
                j = d % 4
                n = 512 if U_P[0] <= d < U_E[0] or U_P[1] <= d < U_E[1] else UNIT
                dve.wait_ge(hi_done, it * step + (d + 1))
                dve.tensor_tensor(wlo[:, j, 0:n], raw[:, j, 0:n], whi[:, j, 0:n].bitcast(f32), ALU.subtract).then_inc(split_done, 1)

            for i in range(NT):
                v = [x[:, 0:KT * T].rearrange("p (k t) -> p k t", t=T)[:, :, P * i:P * i + tok(i)] for x in (xlo, xT, xhi)]
                dve.wait_ge(xhi_ok, i + 1)
                dve.tensor_tensor(v[0], v[1], v[2].bitcast(f32), ALU.subtract).then_inc(xlo_ok, 1)
                if i == 1:
                    lo(0)
                    dve.wait_ge(ws_t, 1)
                    dve.tensor_copy(cols[:, :], ps[:, 0, 0:NCOL]).then_inc(cols_ok, 1)
                    dve.tensor_copy(wst[:, :, :], ps[:, 1, :].rearrange("p (h t) -> p h t", h=NH)).then_inc(ws_cp, 1)
            dve.wait_ge(xhi_ok, NT + 1)
            dve.tensor_tensor(xlo[:, KT * T:], xT[:, KT * T:], xhi[:, KT * T:].bitcast(f32), ALU.subtract).then_inc(xlo_ok, 1)
            for d in range(1, 4):
                lo(d)
            dve.wait_ge(ws_ld, 32)
            dve.memset(bsx[:, :, :].bitcast(f32), 0.0)
            dve.tensor_copy(bss[:, :, 0:P], bsrc[:, :, :])
            for h in range(NH):
                ins = dve.tensor_copy(bss[:, h, P:].rearrange("o (b t) -> o b t", t=SB),
                                      bsrc[:, h, 0:SB].unsqueeze(1).to_broadcast([1, RB, SB]))
            ins.then_inc(bs_ok, 1)
            dve.wait_ge(bsh_ok, 1)
            dve.tensor_tensor(bsl[:, :, :], bss[:, :, :], bsx[0:1, :, :].bitcast(f32), ALU.subtract).then_inc(bsl_ok, 1)

            def v_stats(n, j, it, step, i):
                dve.wait_ge(vg_done, it * (NT * step) + (NT * n + i + 1))
                dve.bn_stats(vstat[:, i, ds(it * step + n, 1), :].rearrange("p a b -> p (a b)"), vst[:, j % 2, i, :]).then_inc(vs_done, 1)

            def v_unit(n, j, it=0, step=0):
                if n >= 2 or step:
                    dve.wait_ge(v_st[j % 2], it * (16 * step) + (n // 2) * 32)
                for i in range(NT):
                    dve.wait_ge(vps_done, it * (NT * step) + (NT * n + i + 1))
                    dve.tensor_tensor(vst[:, j % 2, i, :], ps[:, (NT * n + i) % 4, 0:256],
                                      bvb[:, ds(it * (256 * step) + 256 * n, 256)], ALU.add).then_inc(vz_done, 1)
                    if i == 2 and n + AHEAD >= 4:
                        lo(n + AHEAD, it, step)
                    if i >= 1:
                        v_stats(n, j, it, step, i - 1)
                v_stats(n, j, it, step, NT - 1)

            dve.wait_ge(bv_ld, 16)
            dve.wait_ge(bsl_ld, 16)
            for j in range(2):
                v_unit(j, j)
            with dve.Fori(0, (VU - 4) // 4) as it:
                for j in range(4):
                    v_unit(2 + j, j, it, 4)
            for n in (VU - 2, VU - 1):
                v_unit(n, n)
            dve.wait_ge(vs_done, NT * VU)
            for i in range(NT):
                ins = dve.bn_aggr(mv[:, i, :], vstat[:, i, :, :].rearrange("p a b -> p (a b)"))
            ch.link(ins)
            dve.tensor_scalar(rstd[:, :], mv[:, :, 1], EPS, None, ALU.add).then_inc(rs_ok, 1)
            dve.wait_ge(sq_ok, 1)
            ch.link(dve.reciprocal(rstd[:, :], rstd[:, :]))
            ch.link(dve.scalar_tensor_tensor(out=nmr[:, :], in0=mv[:, :, 0], scalar=-1.0, in1=rstd[:, :], op0=ALU.mult, op1=ALU.mult))

            def v_norm(i):
                t = tok(i)
                ch.link(dve.tensor_scalar(vc[0:t, i, :], vc[0:t, i, :], rstd[0:t, i:i + 1], nmr[0:t, i:i + 1], ALU.mult, ALU.add))
                ch.link(dve.tensor_tensor(vc[0:t, i, :], vc[0:t, i, :], gb[0:t, 0, :], ALU.mult))
                dve.tensor_tensor(vc[0:t, i, :], vc[0:t, i, :], gb[0:t, 1, :], ALU.add).then_inc(vn_ok, 1)

            def gate_product(r, fl, it, step, split):
                q = it * (ROUND * step) + (ROUND * r + fl)
                dve.wait_ge(u_done, q + 1)
                dve.wait_ge(sg_done, q + 1)
                b = 4 + 2 * (fl % 2)
                dve.tensor_tensor(gf[:, fl % 2, 0:TP], gf[:, fl % 2, 0:TP], ps[:, b, :], ALU.mult)
                dve.tensor_tensor(gf[:, fl % 2, TP:T], gf[:, fl % 2, TP:T], ps[:, b + 1, 0:TS], ALU.mult).then_inc(gm_done, 1)
                if fl % 2 == 0:
                    split(fl // 2)
                g_low(q, fl)

            def g_low(q, fl):
                dve.wait_ge(gh_done, q + 1)
                dve.tensor_tensor(glo[:, fl, :], gf[:, fl % 2, :], ghi[:, fl, :].bitcast(f32), ALU.subtract).then_inc(gl_done, 1)

            def add_out(m0, o0, mo, it=0, step=0):
                dve.wait_ge(mt_done, it * (12 * step) + (m0 + 4 + mo + 1))
                if o0 or step:
                    dve.wait_ge(o_done, it * (KT * step) + (o0 - KT + mo + 1))
                x = halves(xk(xT, mo, 0, T))
                dve.tensor_tensor(x, x, pair(mo % 2), ALU.add).then_inc(o_done, 1)

            def a_round(r, it, step, split, norm=True):
                for fl in range(ROUND):
                    gate_product(r, fl, it, step, split)
                for mo in range(KT):
                    if mo == 2:
                        split(2)
                    if mo == 6:
                        split(3)
                    if norm and 2 <= mo < 2 + NT:
                        if mo == 2:
                            dve.wait_ge(vc_ld, it * (64 * step) + 64 * (r + 2))
                        v_norm(mo - 2)
                    add_out(M_A + 12 * r, KT * r, mo, it, step)

            dve.wait_ge(vc_ld, 64)
            for i in range(NT):
                v_norm(i)
            ch.link(dve.tensor_scalar(xT[:, :], xT[:, :], ALPHA, None, ALU.mult))
            a_round(0, 0, 0, lambda j: lo(U_A + j + AHEAD))
            with dve.Fori(0, AR - 2) as it:
                ch.enter(it, 2 * NT)
                a_round(1, it, 1, lambda j: lo(U_A + 4 + j + AHEAD, it, 4))
            ch.leave(AR - 2)
            a_round(AR - 1, 0, 0, lambda j: lo(U_P[0] - 4 + j + AHEAD), norm=False)

            def rstd_of(i, n):
                dve.wait_ge(sq_ok, 1 + n)
                ch.link(dve.reciprocal(rstd[:, i:i + 1], rstd[:, i:i + 1]))
                dve.scalar_tensor_tensor(out=nmr[:, i:i + 1], in0=mv[:, i, 0:1], scalar=-1.0, in1=rstd[:, i:i + 1],
                                         op0=ALU.mult, op1=ALU.mult).then_inc(rs_ok, 1)

            def scale_of(i, n):
                dve.wait_ge(nz_ok, n)
                dve.tensor_tensor(xtok[:, i, :], xtok[:, i, :], lnp[:, 0, :], ALU.mult).then_inc(ng_ok, 1)

            def first_max(src, oh, mx):
                ch.link(dve.tensor_reduce(out=s5[:, mx, :], in_=src, op=ALU.max, axis=AX.X))
                ch.link(dve.tensor_tensor(oh, src, s5[:, mx, :].unsqueeze(2).to_broadcast([P, NT, 4]), ALU.is_equal))
                ch.link(dve.tensor_tensor(oh, oh, minus4, ALU.mult))
                ch.link(dve.tensor_reduce(out=s5[:, 7, :], in_=oh, op=ALU.min, axis=AX.X))
                ch.link(dve.tensor_tensor(oh, minus4, s5[:, 7, :].unsqueeze(2).to_broadcast([P, NT, 4]), ALU.is_equal))

            for l in range(DEPTH):
                n1 = 2 * NT * l
                dve.wait_ge(ln_ld, 32 * (l + 1))
                if l:
                    dve.wait_ge(vs_done, NT * VU)

                def stats_of(i):
                    dve.wait_ge(tr_done, TR_N1[l] + i + 1)
                    b = turned_bank(TR_N1[l] + i)
                    for h in range(2):
                        ins = dve.bn_stats(vstat[:, i, h, :], ps[:, b + h, :])
                    ch.link(ins)
                    dve.bn_aggr(mv[:, i, :], vstat[:, i, 0:2, :].rearrange("p a b -> p (a b)")).then_inc(st_ok, 1)

                stats_of(0)
                stats_of(1)
                rstd_of(0, n1 + 1)
                rstd_of(1, n1 + 2)
                scale_of(0, n1 + 1)
                for i in range(NT):
                    dve.wait_ge(ph_ok, NT * l + i + 1)
                    dve.tensor_tensor(pTlo[:, :, P * i:P * i + tok(i)],
                                      ps[:, i % 4, 0:2 * P].rearrange("p (k t) -> p k t", t=P)[:, :, 0:tok(i)],
                                      pThi[:, :, P * i:P * i + tok(i)].bitcast(f32), ALU.subtract).then_inc(pl_ok, 1)
                lo(U_P[l] + AHEAD)
                for i in range(2, NT + 1):
                    if i < NT:
                        stats_of(i)
                    if i > 2:
                        rstd_of(i - 1, n1 + i)
                    scale_of(i - 1, n1 + i)
                lo(U_E[l])
                lo(U_E[l] + 1)
                dve.wait_ge(wr_ld, 64 * (l + 1))
                dve.wait_ge(r_mm, NT * (l + 1))
                ch.link(dve.tensor_tensor(lg[:, :, :], ps[:, 0, 0:32 * NT].rearrange("p (t c) -> p t c", c=32)[:, :, 0:20],
                                          br[:, :].unsqueeze(1).to_broadcast([P, NT, 20]), ALU.add))
                minus4 = ovw[:, 5, 0:4].unsqueeze(1).to_broadcast([P, NT, 4])
                ch.link(dve.tensor_scalar(ovw[:, 5, 0:4], iota[:, 0:4], -4.0, None, ALU.add))
                dve.memset(m16[TS:P, 4, 0:1], 0.0).then_inc(m_ok, 1)
                gl = lg[:, :, 0:4]
                el = lg[:, :, 4:20].rearrange("p t (g j) -> p t g j", g=4)
                first_max(gl, ohg[:, :, :], 0)
                dve.tensor_tensor(r4[:, :, :], gl, s5[:, 0, :].unsqueeze(2).to_broadcast([P, NT, 4]), ALU.subtract).then_inc(r_ex, 1)
                ch.link(dve.tensor_tensor(t16[:, :, :, :], el, ohg[:, :, :].unsqueeze(3).to_broadcast([P, NT, 4, 4]), ALU.mult))
                ch.link(dve.tensor_reduce(out=ein[:, :, :], in_=t16.rearrange("p t g j -> p t j g"), op=ALU.add, axis=AX.X))
                first_max(ein[:, :, :], oh1[:, :, :], 1)
                ch.link(dve.scalar_tensor_tensor(out=ein[:, :, :], in0=oh1[:, :, :], scalar=-3.0e38, in1=ein[:, :, :], op0=ALU.mult, op1=ALU.add))
                first_max(ein[:, :, :], oh2[:, :, :], 2)
                dve.tensor_tensor(s5[:, 3, :], s5[:, 2, :], s5[:, 1, :], ALU.subtract).then_inc(r_ex, 1)
                for k, oh in enumerate((oh1, oh2)):
                    ins = dve.tensor_tensor(oh16[k], ohg[:, :, :].unsqueeze(3).to_broadcast([P, NT, 4, 4]),
                                            oh[:, :, :].unsqueeze(2).to_broadcast([P, NT, 4, 4]), ALU.mult)
                ch.link(ins)
                ch.link(dve.tensor_tensor(m16[:, :, :], oh16[0].rearrange("p t g j -> p t (g j)"), oh16[1].rearrange("p t g j -> p t (g j)"), ALU.add))
                ch.link(dve.memset(m16[TS:P, 4, :], 0.0))
                ch.link(dve.memset(mpre[:, 0, :], 0.0))
                for i in range(NT):
                    ins = dve.tensor_tensor(mpre[:, i + 1, :], mpre[:, i, :], m16[:, i, :], ALU.add)
                    if i < NT - 1:
                        ch.link(ins)
                ins.then_inc(m_ok, 1)
                dve.wait_ge(r_ex_ok, 2 * (l + 1))
                ch.link(dve.tensor_reduce(out=s5[:, 4, :], in_=r4[:, :, :], op=ALU.add, axis=AX.X))
                ch.link(dve.scalar_tensor_tensor(out=s5[:, 5, :], in0=s5[:, 3, :], scalar=1.0, in1=s5[:, 4, :], op0=ALU.add, op1=ALU.mult))
                ch.link(dve.reciprocal(wtop[:, 0, :], s5[:, 5, :]))
                ch.link(dve.tensor_tensor(wtop[:, 1, :], wtop[:, 0, :], s5[:, 3, :], ALU.mult))
                dve.wait_ge(rank_ok, l + 1)
                rank = ps[:, 7, 0:NT * NE].rearrange("p (t e) -> p t e", e=NE)
                cnt = ps[:, 7, NT * NE:(NT + 1) * NE]
                ch.link(dve.memset(ovw[:, 0:4, 0:8], 0.0))
                ch.link(dve.tensor_scalar(ovw[:, 0, 8:24], cnt, 128.0, None, ALU.is_gt))
                for n in (256.0, 384.0, 512.0):
                    ch.link(dve.scalar_tensor_tensor(out=ovw[:, 0, 8:24], in0=cnt, scalar=n, in1=ovw[:, 0, 8:24], op0=ALU.is_gt, op1=ALU.add))
                a = 0
                for step, b in ((1, 1), (2, 2), (4, 1), (8, 2)):
                    ch.link(dve.tensor_tensor(ovw[:, b, 8:24], ovw[:, a, 8:24], ovw[:, a, 8 - step:24 - step], ALU.add))
                    a = b
                incl = ovw[:, 2, 8:24]
                ch.link(dve.tensor_tensor(ovw[:, 3, 8:24], incl, ovw[:, 0, 8:24], ALU.subtract))
                ch.link(dve.tensor_scalar(ovw[:, 3, 8:24], ovw[:, 3, 8:24], 128.0, float(NE * CAP - CAP), ALU.mult, ALU.add))
                ch.link(dve.tensor_tensor(ovw[:, 3, 8:24], ovw[:, 3, 8:24], iota_e[:, :], ALU.subtract))
                ch.link(dve.tensor_scalar(post[:, :, :], rank, 128.0, None, ALU.is_ge))
                ch.link(dve.tensor_tensor(post[:, :, :], post[:, :, :], ovw[:, 3, 8:24].unsqueeze(1).to_broadcast([P, NT, NE]), ALU.mult))
                ch.link(dve.tensor_tensor(post[:, :, :], post[:, :, :], rank, ALU.add))
                ch.link(dve.tensor_tensor(post[:, :, :], post[:, :, :], iota_e[:, :].unsqueeze(1).to_broadcast([P, NT, NE]), ALU.add))
                for k in range(2):
                    ch.link(dve.tensor_tensor(t16.rearrange("p t g j -> p t (g j)"), oh16[k].rearrange("p t g j -> p t (g j)"), post[:, :, :], ALU.mult))
                    ch.link(dve.tensor_reduce(out=pmd[:, 0, NT * k:NT * k + NT], in_=t16.rearrange("p t g j -> p t (g j)"), op=ALU.add, axis=AX.X))
                dve.tensor_copy(pos_u[:, :, :].rearrange("p t k -> p k t"), pmd[:, 0, :].rearrange("p (k t) -> p k t", k=2)).then_inc(idx_ok, 1)
                ch.link(dve.tensor_copy(posi[:, 0, :], pmd[:, 0, :]))
                ch.link(dve.tensor_single_scalar(posi[:, 1, :], posi[:, 0, :], CAP - 1, op=ALU.bitwise_and))
                ch.link(dve.tensor_single_scalar(posi[:, 2, :], posi[:, 0, :], 7, op=ALU.arith_shift_right))
                ch.link(dve.tensor_copy(pmd[:, 1:3, :], posi[:, 1:3, :]))
                for n in range(2 * NT):
                    if n >= 2:
                        dve.wait_ge(ab_used, 2 * NT * l + n - 1)
                    dve.tensor_scalar(amat[:, n % 2, :], iota[:, :], pmd[:, 1, n:n + 1], None, ALU.is_equal)
                    dve.tensor_scalar(bmat[:, n % 2, :], iota[:, 0:SLOT_TILES], pmd[:, 2, n:n + 1],
                                      tokid[:, n % NT:n % NT + 1], ALU.is_equal, ALU.mult).then_inc(ab_ok, 1)
                ch.link(dve.tensor_tensor(wide[0:1, :, :], incl[0:1].unsqueeze(1).to_broadcast([1, OVF, NE]),
                                          iota[0:1, 0:OVF].unsqueeze(2).to_broadcast([1, OVF, NE]), ALU.is_le))
                ch.link(dve.tensor_reduce(out=ovw[0:1, 4, 0:OVF], in_=wide[0:1, :, :], op=ALU.add, axis=AX.X))
                dve.tensor_scalar(ovf_e[:, :], ovw[0:1, 4, 0:OVF], float(NE - 1), None, ALU.min)
                dve.tensor_copy(n_ovf[:, :], incl[0:1, NE - 1:NE]).then_inc(idx_ok, 1)
                dve.wait_ge(ab_used, 2 * NT * (l + 1))
                dve.tensor_copy(idx[:, :], ps[:, 6, 0:SLOT_TILES]).then_inc(idx_ok, 1)

                def xT_lo(s, it=0, step=0):
                    q = it * (2 * step) + 2 * (NE * l + s)
                    for b in range(2):
                        dve.wait_ge(eth_ok, q + (b + 1))
                        dve.tensor_tensor(eTl[:, 512 * b:512 * b + 512], ps[:, 2 + b, :], eTh[:, 512 * b:512 * b + 512].bitcast(f32),
                                          ALU.subtract).then_inc(etl_ok, 1)

                def expert_lo(e, it, step):
                    if e < EU:
                        lo(U_E[l] + e, it, 3 * step)

                def moe_step(s, it=0, step=0):
                    e = 3 * s + 2
                    expert_lo(e, it, step)
                    expert_lo(e + 1, it, step)
                    if s < NE:
                        q = it * step + (NE * l + s)
                        dve.wait_ge(si_ok, q + 1)
                        if l or s or step:
                            dve.wait_ge(at_ok, q)
                        dve.tensor_tensor(act_a[:, 1, :], act_a[:, 0, :], ps[:, 0, F:2 * F], ALU.mult).then_inc(a_ok, 1)
                    if s < NE - 1:
                        xT_lo(s + 1, it, step)
                        expert_lo(e + 2, it, step)
                    if s < NE:
                        dve.wait_ge(ath_ok, q + 1)
                        dve.tensor_tensor(aTl[:, :], ps[:, 1, 0:F], aTh[:, :].bitcast(f32), ALU.subtract).then_inc(atl_ok, 1)

                xT_lo(0)
                moe_step(0)
                moe_step(1)
                with dve.Fori(0, 3) as it:
                    for s in range(2, 6):
                        moe_step(s, it, 4)
                for s in range(NE - 2, NE + 1):
                    moe_step(s)
                n = dve.value_load(n_ovf[0:1, 0:1], min_val=0, max_val=OVF)
                with dve.If(n > 0):
                    o = ov[l]
                    with dve.Fori(0, OVF) as i:
                        dve.wait_ge(o["silu"], i + 1)
                        dve.tensor_tensor(act_a[:, 1, :], act_a[:, 0, :], ps[:, 0, F:2 * F], ALU.mult).then_inc(o["a"], 1)
                for j in range(AHEAD):
                    lo(U_G[l] + j)
                n2 = n1 + NT
                dve.wait_ge(xs_ok, l + 1)
                for i in range(NT + 1):
                    if i < NT:
                        t = tok(i)
                        dve.wait_ge(yg_ld[i % 4], 32 * ((2 if i % 4 == 0 else 1) * l + i // 4 + 1))
                        if i >= 3:
                            dve.wait_ge(cb_ok, 2 * l + i - 2)
                        for k in range(0 if i < 3 else 1, 2):
                            ch.link(dve.scalar_tensor_tensor(out=xtok[0:t, i, :], in0=yrows(i, t, k), scalar=wtop[0:t, k, i:i + 1],
                                                             in1=xtok[0:t, i, :], op0=ALU.mult, op1=ALU.add))
                        for h in range(2):
                            ins = dve.bn_stats(vstat[:, i, h, :], xtok[:, i, 512 * h:512 * h + 512])
                        ch.link(ins)
                        dve.bn_aggr(mv[:, i, :], vstat[:, i, 0:2, :].rearrange("p a b -> p (a b)")).then_inc(st_ok, 1)
                    if i >= 1:
                        rstd_of(i - 1, n2 + i)
                dve.wait_ge(tr_free, TF_N2[l] + NT)
                for k in range(KT):
                    x, c = xk(xT, k, 0, T), KT * l + k
                    dve.tensor_scalar(x, x, cols[:, C_G2 + c:C_G2 + c + 1], cols[:, C_B2 + c:C_B2 + c + 1], ALU.mult, ALU.add).then_inc(xT_ok, 1)

                def x_lo(n):
                    for k in range(KT):
                        dve.wait_ge(xhi_ok, n + k + 1)
                        dve.tensor_tensor(xk(xlo, k, 0, T), xk(xT, k, 0, T), xk(xhi, k, 0, T).bitcast(f32), ALU.subtract).then_inc(xlo_ok, 1)

                x_lo(NT + 1 + 2 * KT * l)
                for j in range(4):
                    if U_G[l] + j + AHEAD < U_END:
                        lo(U_G[l] + j + AHEAD)
                    for m in range(2):
                        mo = 2 * j + m
                        dve.wait_ge(sg_ok, KT * l + mo + 1)
                        ch.link(dve.tensor_tensor(sgm[:, m, :], sgm[:, m, :], ppT[:, mo, :], ALU.mult))
                        dve.tensor_tensor(xk(xT, mo, 0, T), xk(xT, mo, 0, T), sgm[:, m, :], ALU.add).then_inc(pe_ok, 1)
                if l == 0:
                    x_lo(NT + 1 + KT)
                    dve.wait_ge(xlo_ok, NT + 1 + 2 * KT)
                    ch.link(dve.tensor_scalar(xT[:, :], xT[:, :], ALPHA, None, ALU.mult))
                    dve.wait_ge(past_t, 1)
                    ch.link(dve.tensor_copy(pastT[:, :, :], ps[:, 6, 0:KT * RB * 2].rearrange("p (k c) -> p k c", k=KT)))
                    for m in range(2):
                        ins = dve.memset(cx[:, m, 0:2], 0.0)
                    ch.link(ins)

                    def conv_tile(f, m):
                        own = cx[:, m, 2 + TP:].rearrange("p (b t) -> p b t", t=2 + SB)
                        dve.tensor_copy(own[:, :, 0:2], pastT[:, f, :].rearrange("p (b w) -> p b w", w=2))
                        for h, (c0, c1) in enumerate(((0, HALF), (HALF, TP))):
                            dve.tensor_tensor(cx[:, m, 2 + c0:2 + c1], c_sb[:, m, c0:c1], ps[:, 2 * m + h, c0 - HALF * h:c1 - HALF * h], ALU.mult)
                        dve.tensor_tensor(own[:, :, 2:], c_sb[:, m, TP:T].rearrange("p (b t) -> p b t", t=SB),
                                          ps[:, 2 * m + 1, TP - HALF:HALF].rearrange("p (b t) -> p b t", t=SB), ALU.mult).then_inc(cx_ok, 1)
                        dve.wait_ge(cx_ok, f + 1)
                        o_p, o_s = conv[:, f, 0:TP], conv[:, f, TP:T].rearrange("p (b t) -> p b t", t=SB)
                        w = [cols[:, C_CW + KT * n + f:C_CW + KT * n + f + 1] for n in range(3)]
                        dve.tensor_scalar(o_p, cx[:, m, 0:TP], w[0], None, ALU.mult)
                        ch.link(dve.tensor_scalar(o_s, own[:, :, 0:SB], w[0], None, ALU.mult))
                        for n in (1, 2):
                            dve.scalar_tensor_tensor(out=o_p, in0=cx[:, m, n:n + TP], scalar=w[n], in1=o_p, op0=ALU.mult, op1=ALU.add)
                            ch.link(dve.scalar_tensor_tensor(out=o_s, in0=own[:, :, n:n + SB], scalar=w[n], in1=o_s, op0=ALU.mult, op1=ALU.add))
                        dve.tensor_copy(last[:, f, 0:2], cx[:, m, TP:TP + 2])
                        dve.tensor_copy(last[:, f, 2:].rearrange("p (b w) -> p b w", w=2), own[:, :, SB:SB + 2]).then_inc(last_ok, 1)

                    for jj in range(4):
                        lo(U_CH + 2 * jj + AHEAD)
                        for m in range(2):
                            dve.wait_ge(c_ok, 2 * jj + m + 1)
                            dve.wait_ge(mt_done, M_CH + 4 * jj + 2 + m + 1)
                            conv_tile(2 * jj + m, m)
                        lo(U_CH + 2 * jj + 1 + AHEAD)
                    for r in range(BR):
                        for fl in range(ROUND):
                            q = ROUND * (AR + r) + fl
                            dve.wait_ge(mt_done, M_B + 12 * r + fl + 1)
                            dve.tensor_tensor(halves(gf[:, fl % 2, :]), halves(conv[:, ROUND * r + fl, :]), pair(fl % 2), ALU.mult).then_inc(gm_done, 1)
                            g_low(q, fl)
                            if fl < 3:
                                lo(U_B + 4 * r + fl + AHEAD)
                        for mo in range(KT):
                            if mo == 6:
                                lo(U_B + 4 * r + 3 + AHEAD)
                            add_out(M_B + 12 * r, KT * (AR + r), mo)

        @block.tensor
        def _(pe):
            def turn_rows(n, src):
                b = turned_bank(n)
                for k in range(KT):
                    ins = pe.transpose(ps[:, b + k // 4, (k % 4) * P:(k % 4) * P + P], src[:, k * P:k * P + P], ident[:, :])
                ins.then_inc(tr_done, 1)

            def turn_cols(n, i):
                b = turned_bank(n)
                for k in range(KT):
                    ins = pe.transpose(ps[:, b + k // 4, (k % 4) * P:(k % 4) * P + P], xk(xT, k, P * i, P), ident[:, :])
                ins.then_inc(tr_done, 1)

            def products(out, terms, opens=True, closes=True):
                for n, (sh, sl, mh, ml) in enumerate(terms):
                    first, final = opens and n == 0, closes and n == len(terms) - 1
                    pe.matmul(out, sh, mh, start=first, stop=False)
                    pe.matmul(out, sh, ml, start=False, stop=False)
                    ins = pe.matmul(out, sl, mh, start=False, stop=final)
                return ins

            def dense_tile(par, j, c0, kn, wview, xh_, xl_, xview, k0=0, k1=None):
                k1 = kn if k1 is None else k1
                for h in range(2):
                    ins = products(ps[:, 2 * par + h, 0:HALF],
                                   [(wview(whi, j, k, c0), wview(wlo, j, k, c0), xview(xh_, k, h), xview(xl_, k, h)) for k in range(k0, k1)],
                                   k0 == 0, k1 == kn)
                return ins

            def xview(x, k, h):
                return xk(x, k, HALF * h, HALF)

            def first_tile(x0):
                for k in range(KT):
                    pe.wait_ge(xlo_ok, x0 + k + 1)
                    ins = dense_tile(0, 0, 0, KT, w8, xhi, xlo, xview, k, k + 1)
                ins.then_inc(mt_done, 1)

            def gview(g, k, h):
                return g[:, k, HALF * h:HALF * h + HALF]

            pe.wait_ge(const_ok, 1)
            pe.wait_ge(x_ld, 32)
            def input_turn(i):
                if i >= 2:
                    pe.wait_ge(tr_free, i - 1)
                turn_rows(TR_IN + i, xtok[:, i, :])

            input_turn(0)
            input_turn(1)
            pe.wait_ge(small_ld, 80)
            pe.wait_ge(ws_ld, 32)
            pe.transpose(ps[:, 0, 0:NCOL], colsrc[:, :], ident[0:NCOL, 0:NCOL])
            for h in range(NH):
                ins = pe.transpose(ps[:, 1, h * P:h * P + P], wsrc[:, h, :], ident[:, :])
            ins.then_inc(ws_t, 1)

            def v_unit(n, j, it=0, step=0):
                pe.wait_ge(split_done, it * step + (n + 1))
                for i in range(NT):
                    if n == 0:
                        if i + 2 < NT:
                            input_turn(i + 2)
                        if i < 2:
                            pe.wait_ge(ws_cp, 1)
                        pe.wait_ge(xlo_ok, i + 1 if i < NT - 1 else NT + 1)
                    q = NT * n + i
                    if q >= 4 or step:
                        pe.wait_ge(vz_done, it * (NT * step) + (q - 3))
                    products(ps[:, q % 4, 0:256],
                             [(xk(xhi, k, P * i, P), xk(xlo, k, P * i, P), w8(whi, j, k, 0, 256), w8(wlo, j, k, 0, 256))
                              for k in range(KT)]).then_inc(vps_done, 1)

            for n in range(4):
                v_unit(n, n)
            with pe.Fori(0, VU // 4 - 1) as it:
                for j in range(4):
                    v_unit(4 + j, j, it, 4)
            pe.wait_ge(vz_done, V_DONE)

            pe.wait_ge(bsl_ld, 16)
            pe.wait_ge(ones_ok, 1)
            pe.wait_ge(blk_ld, 16 * RB)

            def spatial(r, fl, it, step):
                q = it * (ROUND * step) + (ROUND * r + fl)
                if fl == 0:
                    pe.wait_ge(vn_ok, it * (NT * step) + NT * (r + 1))
                if r or step or fl >= 2:
                    pe.wait_ge(gm_done, q - 1)
                b = 4 + 2 * (fl % 2)
                half = it * (2 * step) + (2 * r + fl // 2)
                h = (half * 11) // 32
                for c in range(4):
                    out = ps[:, b, P * c:P * c + P]
                    pe.matmul(out, ones_r[:, :], bsx[:, ds(h, 1), 0:P].rearrange("p a t -> p (a t)"), start=True, stop=False)
                    pe.matmul(out, vc[:, c, P * fl:P * fl + P], wst[:, ds(h, 1), :].rearrange("p a t -> p (a t)"), start=False, stop=True)
                out = ps[:, b + 1, 0:TS]
                pe.matmul(out, ones_r[:, :], bsx[:, ds(h, 1), P:].rearrange("p a t -> p (a t)"), start=True, stop=False)
                pe.matmul(out, vc[0:TS, 4, P * fl:P * fl + P], wss[:, ds(h, 1), :].rearrange("p a t -> p (a t)"),
                          start=False, stop=True).then_inc(sg_done, 1)

            def a_round(r, it, step):
                def u_tile(fl):
                    if fl % 2 == 0:
                        pe.wait_ge(split_done, it * (4 * step) + (U_A + 4 * r + fl // 2 + 1))
                    if fl >= 2:
                        pe.wait_ge(u_done, it * (ROUND * step) + (ROUND * r + fl - 1))
                    elif r or step:
                        pe.wait_ge(o_done, it * (KT * step) + (KT * r - 1 + fl))
                    dense_tile(fl % 2, fl // 2, P * (fl % 2), KT, w8, xhi, xlo, xview).then_inc(mt_done, 1)

                u_tile(0)
                u_tile(1)
                spatial(r, 0, it, step)
                spatial(r, 1, it, step)
                u_tile(2)
                spatial(r, 2, it, step)
                u_tile(3)
                spatial(r, 3, it, step)
                out_tiles(it * (ROUND * step) + ROUND * (r + 1), u_done, it * (ROUND * step) + ROUND * (r + 1),
                          it * (KT * step) + KT * r, it * (4 * step) + (U_A + 4 * r + 2))

            def out_tiles(gl_n, pair_sem, pair_n, o0, d):
                pe.wait_ge(gl_done, gl_n - 1)
                pe.wait_ge(split_done, d + 1)
                for mo in range(2):
                    pe.wait_ge(pair_sem, pair_n + (mo - 1))
                    dense_tile(mo, 2, P * mo, ROUND, w4, ghi, glo, gview, 0, ROUND - 1)
                pe.wait_ge(gl_done, gl_n)
                for mo in range(2):
                    dense_tile(mo, 2, P * mo, ROUND, w4, ghi, glo, gview, ROUND - 1, ROUND).then_inc(mt_done, 1)
                for mo in range(2, KT):
                    if mo == 4:
                        pe.wait_ge(split_done, d + 2)
                    pe.wait_ge(o_done, o0 + (mo - 1))
                    dense_tile(mo % 2, 2 + mo // 4, P * (mo % 4), ROUND, w4, ghi, glo, gview).then_inc(mt_done, 1)

            a_round(0, 0, 0)
            with pe.Fori(0, AR - 1) as it:
                a_round(1, it, 1)

            for l in range(DEPTH):
                o_all = KT * (AR + BR * l)
                pe.wait_ge(o_done, o_all)

                def n1_turn(i):
                    if i >= 2:
                        pe.wait_ge(nz_ok, 2 * NT * l + i - 1)
                    turn_cols(TR_N1[l] + i, i)

                n1_turn(0)
                n1_turn(1)
                pe.wait_ge(p_ld, 32 * (l + 1))
                for i in range(NT):
                    if i == 4:
                        pe.wait_ge(pl_ok, NT * l + 1)
                    for k in range(2):
                        ins = pe.transpose(ps[:, i % 4, k * P:k * P + tok(i)], p_tok[0:tok(i), i, k * P:k * P + P], ident[0:tok(i), 0:tok(i)])
                    ins.then_inc(p_turn, 1)

                def pview(p, k, h):
                    return p[:, k, HALF * h:HALF * h + HALF]

                def proj(mo):
                    if mo % 2 == 0:
                        pe.wait_ge(split_done, U_P[l] + mo // 2 + 1)
                    if mo >= 2:
                        pe.wait_ge(pp_done, KT * l + mo - 1)
                    dense_tile(mo % 2, mo // 2, P * (mo % 2), 2, w8, pThi, pTlo, pview).then_inc(mt_done, 1)

                def router_turn(i):
                    if i:
                        pe.wait_ge(r_cp, NT * l + i)
                    else:
                        pe.wait_ge(pp_done, KT * l + 4)
                        pe.wait_ge(wr_ld, 64 * (l + 1))
                    pe.wait_ge(nb_ok, NT * l + i + 1)
                    for k in range(KT):
                        ins = pe.transpose(ps[:, 2 + k // 4, (k % 4) * P:(k % 4) * P + P], xtok[:, i, k * P:k * P + P], ident[:, :])
                    ins.then_inc(r_turn, 1)

                def logits(i):
                    pe.wait_ge(r_cp, NT * l + i + 1)
                    for k in range(KT):
                        ins = pe.matmul(ps[:, 0, 32 * i:32 * i + 20], x1T[i % 2][:, k, :], wr[:, k, :], start=(k == 0), stop=(k == KT - 1))
                    ins.then_inc(r_mm, 1)

                n1_turn(2)
                n1_turn(3)
                pe.wait_ge(pl_ok, NT * (l + 1))
                proj(0)
                proj(1)
                proj(2)
                proj(3)
                n1_turn(4)
                router_turn(0)
                for i in range(1, NT):
                    router_turn(i)
                    logits(i - 1)
                logits(NT - 1)
                pe.wait_ge(m_ok, 2 * l + 1)
                for mo in range(4, 7):
                    proj(mo)
                pe.wait_ge(m_ok, 2 * l + 2)
                pe.matmul(ps[:, 7, 0:NE * NT], below[:, :], m16[:, :, :].rearrange("p t e -> p (t e)"), start=True, stop=False)
                pe.matmul(ps[:, 7, 0:NE * NT], ones[:, :], mpre[:, 0:NT, :].rearrange("p t e -> p (t e)"), start=False, stop=True)
                pe.matmul(ps[:, 7, NE * NT:NE * NT + NE], ones[:, :], mpre[:, NT, :], start=True, stop=True).then_inc(rank_ok, 1)
                proj(7)
                for n in range(2 * NT):
                    pe.wait_ge(ab_ok, 2 * NT * l + n + 1)
                    ins = pe.matmul(ps[:, 6, 0:SLOT_TILES], amat[:, n % 2, :], bmat[:, n % 2, :], start=(n == 0), stop=(n == 2 * NT - 1))
                    ins.then_inc(ab_used, 1)

                def turn_slots(s, it=0, step=0, par=0):
                    pe.wait_ge(xg_ld[par], it * (8 * step) + 16 * ((NE // 2) * l + s // 2 + 1))
                    if l or s or step:
                        pe.wait_ge(etl_ok, it * (2 * step) + 2 * (NE * l + s))
                    for k in range(KT):
                        ins = pe.transpose(ps[:, 2 + k // 4, (k % 4) * P:(k % 4) * P + P], xg[:, par, k * P:k * P + P], ident[:, :])
                        if k % 4 == 3:
                            ins.then_inc(xtp, 1)

                def gate_up(s, it=0, step=0):
                    q = it * step + (NE * l + s)
                    pe.wait_ge(etl_ok, q * 2 + 2)
                    if l or s or step:
                        pe.wait_ge(a_ok, q)
                    for a in range(2):
                        e = gu_unit(s) + a
                        pe.wait_ge(split_done, it * (3 * step) + (U_E[l] + e + 1))
                        for k in range(4):
                            xs = [x[:, (4 * a + k) * P:(4 * a + k) * P + P] for x in (eTh, eTl)]
                            ws = [w[:, e % 4, 512 * k:512 * k + 512] for w in (whi, wlo)]
                            pe.matmul(ps[:, 0, :], xs[0], ws[0], start=(a == 0 and k == 0), stop=False)
                            pe.matmul(ps[:, 0, :], xs[0], ws[1], start=False, stop=False)
                            ins = pe.matmul(ps[:, 0, :], xs[1], ws[0], start=False, stop=(a == 1 and k == 3))
                        ins.then_inc(eu_used, 1)

                def down(s, it=0, step=0):
                    q = it * step + (NE * l + s)
                    pe.wait_ge(atl_ok, q + 1)
                    if l or s or step:
                        pe.wait_ge(y_cp, q)
                    e = dn_unit(s)
                    pe.wait_ge(split_done, it * (3 * step) + (U_E[l] + e + 1))
                    for a in range(2):
                        for h in range(2):
                            out = ps[:, 4 + h, :]
                            th, tl = aTh[:, P * a:P * a + P], aTl[:, P * a:P * a + P]
                            wh, wl = [w[:, e % 4, D * a + 512 * h:D * a + 512 * h + 512] for w in (whi, wlo)]
                            pe.matmul(out, th, wh, start=(a == 0), stop=False)
                            pe.matmul(out, th, wl, start=False, stop=False)
                            ins = pe.matmul(out, tl, wh, start=False, stop=(a == 1))
                    ins.then_inc(eu_used, 1)

                def turn_act(s, it=0, step=0):
                    q = it * step + (NE * l + s)
                    pe.wait_ge(a_ok, q + 1)
                    if l or s or step:
                        pe.wait_ge(atl_ok, q)
                    for c in range(2):
                        ins = pe.transpose(ps[:, 1, P * c:P * c + P], act_a[:, 1, P * c:P * c + P], ident[:, :])
                    ins.then_inc(at_ok, 1)

                def moe_step(s, it=0, step=0):
                    if s < NE:
                        gate_up(s, it, step)
                    if s < NE - 1:
                        turn_slots(s + 1, it, step, (s + 1) % 2)
                    if s >= 1 or step:
                        down(s - 1, it, step)
                    if s < NE:
                        turn_act(s, it, step)

                pe.wait_ge(pp_done, KT * (l + 1))
                pe.wait_ge(idx_ok, 3 * (l + 1))
                turn_slots(0)
                moe_step(0)
                moe_step(1)
                with pe.Fori(0, 3) as it:
                    for s in range(2, 6):
                        moe_step(s, it, 4)
                for s in range(NE - 2, NE + 1):
                    moe_step(s)
                n = pe.value_load(n_ovf[0:1, 0:1], min_val=0, max_val=OVF)
                with pe.If(n > 0):
                    o = ov[l]
                    wgu = raw[:, 0:2, :].rearrange("p a (k c) -> p (a k) c", c=2 * F)
                    wdn = raw[:, 2, :].rearrange("p (k c) -> p k c", c=D)
                    pe.wait_ge(y_cp, NE * (l + 1))
                    with pe.Fori(0, OVF) as i:
                        pe.wait_ge(ovx_ld[l], i * 16 + 16)
                        for k in range(KT):
                            ins = pe.transpose(ps[:, 2 + k // 4, (k % 4) * P:(k % 4) * P + P], xg[:, 0, k * P:k * P + P], ident[:, :])
                        ins.then_inc(o["turned"], 1)
                        pe.wait_ge(o["copied"], i + 1)
                        pe.wait_ge(ov_ld[l], i * 48 + 48)
                        for k in range(KT):
                            ins = pe.matmul(ps[:, 0, :], eTf[:, k * P:k * P + P], wgu[:, k, :], start=(k == 0), stop=(k == KT - 1))
                        ins.then_inc(o["gu"], 1)
                        pe.wait_ge(o["a"], i + 1)
                        for c in range(2):
                            ins = pe.transpose(ps[:, 1, P * c:P * c + P], act_a[:, 1, P * c:P * c + P], ident[:, :])
                        ins.then_inc(o["aturned"], 1)
                        pe.wait_ge(o["acopied"], i + 1)
                        for h in range(2):
                            for k in range(2):
                                ins = pe.matmul(ps[:, 4 + h, :], aTf[:, k * P:k * P + P], wdn[:, k, 512 * h:512 * h + 512],
                                                start=(k == 0), stop=(k == 1))
                        ins.then_inc(o["y"], 1)
                        pe.wait_ge(o["ycopied"], i + 1)
                pe.wait_ge(y_cp, NE * (l + 1))
                for i in range(NT):
                    if i >= 2:
                        pe.wait_ge(tr_free, TF_N2[l] + i - 1)
                    pe.wait_ge(nz_ok, 2 * NT * l + NT + i + 1)
                    turn_rows(TR_N2[l] + i, xtok[:, i, :])
                pe.wait_ge(atl_ok, NE * (l + 1))
                for mo in range(KT):
                    if mo % 2 == 0:
                        pe.wait_ge(split_done, U_G[l] + mo // 2 + 1)
                    if mo >= 2:
                        pe.wait_ge(sg_ok, KT * l + mo - 1)
                    if mo:
                        dense_tile(mo % 2, mo // 2, P * (mo % 2), KT, w8, xhi, xlo, xview).then_inc(mt_done, 1)
                    else:
                        first_tile(NT + 1 + 2 * KT * l)
                if l == 0:
                    pe.wait_ge(past_ld, 16)
                    for k in range(KT):
                        ins = pe.transpose(ps[:, 6, 2 * RB * k:2 * RB * k + 2 * RB], past[:, k * P:k * P + P], ident[0:2 * RB, 0:2 * RB])
                    ins.then_inc(past_t, 1)
                    for jj in range(4):
                        for part in range(2):
                            pe.wait_ge(split_done, U_CH + 2 * jj + part + 1)
                            for m in range(2):
                                if part:
                                    pe.wait_ge(c_ok, 2 * jj + m + 1)
                                elif jj:
                                    pe.wait_ge(cx_ok, 2 * jj - 1 + m)
                                else:
                                    pe.wait_ge(sg_ok, KT)
                                if jj or part or m:
                                    dense_tile(m, (2 * jj + part) % 4, P * m, KT, w8, xhi, xlo, xview).then_inc(mt_done, 1)
                                else:
                                    first_tile(NT + 1 + KT)
                    for r in range(BR):
                        for fl in range(ROUND):
                            if fl % 2 == 0:
                                pe.wait_ge(split_done, U_B + 4 * r + fl // 2 + 1)
                            if fl >= 2:
                                pe.wait_ge(gm_done, ROUND * (AR + r) + fl - 1)
                            elif r:
                                pe.wait_ge(o_done, KT * (AR + r) - 1 + fl)
                            else:
                                pe.wait_ge(cx_ok, KT - 1 + fl)
                            dense_tile(fl % 2, fl // 2, P * (fl % 2), KT, w8, xhi, xlo, xview).then_inc(mt_done, 1)
                        out_tiles(ROUND * (AR + r + 1), gm_done, ROUND * (AR + r + 1), KT * (AR + r), U_B + 4 * r + 2)
                        if r == 0:
                            pe.wait_ge(last_ok, KT)
                            for k in range(KT):
                                ins = pe.transpose(ps[0:18, 6 + k // 4, (k % 4) * P:(k % 4) * P + P], last[:, k, :], ident[:, :])
                            ins.then_inc(last_t, 1)
                    pe.wait_ge(last_cp, 1)
            pe.wait_ge(pe_ok, 2 * KT)
            for i in range(NT):
                if i >= 2:
                    pe.wait_ge(out_cp, i - 1)
                turn_cols(TR_OUT + i, i)


_OUTS = [((1, TP, D), "float32"), ((RB, SB, D), "float32"), ((1, 1, P, AW), "float32"),
         ((1, RB, SB, AW), "float32"), ((1, 1, 2, D), "float32"), ((1, RB, 2, D), "float32")]


def kernel(**inputs):
    import numpy as _np
    import concourse.bacc as _bacc
    from concourse import mybir as _mybir
    from concourse.bass_utils import run_bass_kernel_spmd as _run

    nc = _bacc.Bacc("TRN2", target_bir_lowering=False, num_devices=1)
    arrays, ins, outs = {}, {}, []
    for name, a in inputs.items():
        a = _np.ascontiguousarray(a)
        arrays[f"in_{name}"] = a
        ins[name] = nc.dram_tensor(f"in_{name}", a.shape, _mybir.dt.from_np(a.dtype), kind="ExternalInput").ap()
    for i, (shape, dtype) in enumerate(_OUTS):
        outs.append(nc.dram_tensor(f"out_{i}", shape, _mybir.dt.from_np(_np.dtype(dtype)), kind="ExternalOutput").ap())
    trunk(nc, ins, outs)
    r = _run(nc, [arrays], core_ids=[0])
    return tuple(r.results[0][f"out_{i}"] for i in range(len(_OUTS)))
```
